# Optimizing a Trainium2 kernel written in Bass

```python
import math
import jax, jax.numpy as jnp
from jax import lax
import numpy as np

D_MODEL = 1024
BATCH = 1
SEQ = 1024
DEPTH = 2
DEC_BATCH = 8
DEC_SEQ = 4
PAST_LEN = 256
PAGE_SIZE = 128

N_MIXERS = 2
N_CONV_LAYERS = (DEPTH + 1) // 2
N_ATTN_LAYERS = DEPTH // 2
N_HEADS = 16
HEAD_DIM = D_MODEL // N_HEADS
CONV_WIDTH = 3
D_FF = 2816
Q_BLOCK = 128
NORM_EPS = 1e-6
SB_BIAS_MEAN = -6.0

kernel_name = "hybrid_shortconv_stickbreaking_convffn_step"

def rmsnorm(x, g):
    xf = x.astype(jnp.float32)
    y = xf * lax.rsqrt(jnp.mean(xf * xf, axis=-1, keepdims=True) + NORM_EPS) * g.astype(jnp.float32)
    return y.astype(x.dtype)

def causal_dwconv(u, prev, w):
    T = u.shape[1]
    ext = jnp.concatenate([prev.astype(u.dtype), u], axis=1)
    y = ext[:, 0:T] * w[0]
    for j in range(1, CONV_WIDTH):
        y = y + ext[:, j:j + T] * w[j]
    return y, ext[:, -(CONV_WIDTH - 1):]

def short_conv_mixer(h, prev, w_in, w_dw, w_out):
    proj = h @ w_in
    b_gate, c_gate, v = jnp.split(proj, 3, axis=-1)
    u = c_gate * v
    uc, st = causal_dwconv(u, prev, w_dw)
    return (b_gate * uc) @ w_out, st

def stick_breaking(q, k, v, q_pos, k_pos, bias):
    scale = 1.0 / math.sqrt(HEAD_DIM)
    z = jnp.einsum('bqhd,bkhd->bhqk', q.astype(jnp.float32), k.astype(jnp.float32)) * scale
    z = z + bias.astype(jnp.float32)[None, :, None, None]
    mask = (k_pos[None, :] < q_pos[:, None])[None, None]
    log_keep = jnp.where(mask, jax.nn.log_sigmoid(-z), 0.0)
    after = lax.cumsum(log_keep, axis=3, reverse=True) - log_keep
    w = jnp.where(mask, jnp.exp(jax.nn.log_sigmoid(z) + after), 0.0)
    o = jnp.einsum('bhqk,bkhd->bqhd', w, v.astype(jnp.float32))
    return o.astype(q.dtype)

def sb_mixer(h, w_qkv, w_o, sb_bias, k_past, v_past, q_pos, k_pos):
    B, T, _ = h.shape
    qkv = (h @ w_qkv).reshape(B, T, 3, N_HEADS, HEAD_DIM)
    q, k, v = qkv[:, :, 0], qkv[:, :, 1], qkv[:, :, 2]
    if k_past is None:
        k_all, v_all = k, v
    else:
        k_all = jnp.concatenate([k_past.astype(k.dtype), k], axis=1)
        v_all = jnp.concatenate([v_past.astype(v.dtype), v], axis=1)
    if T % Q_BLOCK == 0:
        n_blk = T // Q_BLOCK
        qb = jnp.moveaxis(q.reshape(B, n_blk, Q_BLOCK, N_HEADS, HEAD_DIM), 1, 0)
        pb = q_pos.reshape(n_blk, Q_BLOCK)
        ob = lax.map(lambda a: stick_breaking(a[0], k_all, v_all, a[1], k_pos, sb_bias), (qb, pb))
        o = jnp.moveaxis(ob, 0, 1).reshape(B, T, D_MODEL)
    else:
        o = stick_breaking(q, k_all, v_all, q_pos, k_pos, sb_bias).reshape(B, T, D_MODEL)
    return o @ w_o, k, v

def conv_ffn(h, prev, w_up, w_dw, b_dw, w_down):
    up = h @ w_up
    g, u = jnp.split(up, 2, axis=-1)
    gc, st = causal_dwconv(g, prev, w_dw)
    a = jax.nn.silu(gc + b_dw) * u
    return a @ w_down, st

def trunk(x, q_pos, k_pos, conv_prev, ffn_prev, k_past, v_past,
          norm_mix, norm_ffn, norm_final, w_sc_in, w_sc_dw, w_sc_out,
          w_qkv, w_o, sb_bias, w_ffn_up, w_ffn_dw, b_ffn_dw, w_ffn_down):
    conv_new, ffn_new, k_new, v_new = [], [], [], []
    for i in range(DEPTH):
        a = i // N_MIXERS
        h = rmsnorm(x, norm_mix[i])
        if i % N_MIXERS == 0:
            y, st = short_conv_mixer(h, conv_prev[a], w_sc_in[a], w_sc_dw[a], w_sc_out[a])
            conv_new.append(st)
        else:
            kp = None if k_past is None else k_past[a]
            vp = None if v_past is None else v_past[a]
            y, kn, vn = sb_mixer(h, w_qkv[a], w_o[a], sb_bias[a], kp, vp, q_pos, k_pos)
            k_new.append(kn)
            v_new.append(vn)
        x = x + y
        h = rmsnorm(x, norm_ffn[i])
        y, st = conv_ffn(h, ffn_prev[i], w_ffn_up[i], w_ffn_dw[i], b_ffn_dw[i], w_ffn_down[i])
        ffn_new.append(st)
        x = x + y
    return (rmsnorm(x, norm_final), jnp.stack(conv_new), jnp.stack(ffn_new),
            jnp.stack(k_new), jnp.stack(v_new))

def setup_inputs(seed: int = 0) -> dict:
    key = jax.random.key(seed)
    ks = jax.random.split(key, 24)
    n_pages = PAST_LEN // PAGE_SIZE
    n_used = DEC_BATCH * n_pages
    n_pool = (5 * n_used + 3) // 4
    nrm = jax.random.normal
    f32 = jnp.float32
    d, w = D_MODEL, CONV_WIDTH
    perm = jax.random.permutation(ks[0], n_pool)[:n_used]
    page_table = perm.reshape(DEC_BATCH, n_pages).astype(jnp.int32)
    return {
        "x_prompt": nrm(ks[1], (BATCH, SEQ, d), f32),
        "x_sample": nrm(ks[2], (DEC_BATCH, DEC_SEQ, d), f32),
        "cache_k": nrm(ks[3], (N_ATTN_LAYERS, n_pool, PAGE_SIZE, N_HEADS, HEAD_DIM), f32),
        "cache_v": nrm(ks[4], (N_ATTN_LAYERS, n_pool, PAGE_SIZE, N_HEADS, HEAD_DIM), f32),
        "state_conv": nrm(ks[5], (N_CONV_LAYERS, DEC_BATCH, w - 1, d), f32),
        "state_ffn": nrm(ks[6], (DEPTH, DEC_BATCH, w - 1, D_FF), f32),
        "page_table": page_table,
        "norm_mix": 1.0 + 0.02 * nrm(ks[7], (DEPTH, d), f32),
        "norm_ffn": 1.0 + 0.02 * nrm(ks[8], (DEPTH, d), f32),
        "norm_final": 1.0 + 0.02 * nrm(ks[9], (d,), f32),
        "w_sc_in": nrm(ks[10], (N_CONV_LAYERS, d, 3 * d), f32) * d ** -0.5,
        "w_sc_dw": nrm(ks[11], (N_CONV_LAYERS, w, d), f32) * w ** -0.5,
        "w_sc_out": nrm(ks[12], (N_CONV_LAYERS, d, d), f32) * d ** -0.5,
        "w_qkv": nrm(ks[13], (N_ATTN_LAYERS, d, 3 * d), f32) * d ** -0.5,
        "w_o": nrm(ks[14], (N_ATTN_LAYERS, d, d), f32) * d ** -0.5,
        "sb_bias": SB_BIAS_MEAN + 0.5 * nrm(ks[19], (N_ATTN_LAYERS, N_HEADS), f32),
        "w_ffn_up": nrm(ks[15], (DEPTH, d, 2 * D_FF), f32) * d ** -0.5,
        "w_ffn_dw": nrm(ks[16], (DEPTH, w, D_FF), f32) * w ** -0.5,
        "b_ffn_dw": 0.01 * nrm(ks[17], (DEPTH, D_FF), f32),
        "w_ffn_down": nrm(ks[18], (DEPTH, D_FF, d), f32) * D_FF ** -0.5,
    }

def reference(x_prompt, x_sample, cache_k, cache_v, state_conv, state_ffn, page_table,
              norm_mix, norm_ffn, norm_final, w_sc_in, w_sc_dw, w_sc_out,
              w_qkv, w_o, sb_bias, w_ffn_up, w_ffn_dw, b_ffn_dw, w_ffn_down):
    bp, tp, _ = x_prompt.shape
    pos_p = jnp.arange(tp, dtype=jnp.int32)
    conv0 = jnp.zeros((N_CONV_LAYERS, bp, CONV_WIDTH - 1, D_MODEL), x_prompt.dtype)
    ffn0 = jnp.zeros((DEPTH, bp, CONV_WIDTH - 1, D_FF), x_prompt.dtype)
    y_prompt, new_conv_prompt, new_ffn_prompt, new_k_prompt, new_v_prompt = trunk(
        x_prompt, pos_p, pos_p, conv0, ffn0, None, None,
        norm_mix, norm_ffn, norm_final, w_sc_in, w_sc_dw, w_sc_out,
        w_qkv, w_o, sb_bias, w_ffn_up, w_ffn_dw, b_ffn_dw, w_ffn_down)

    bs, ts, _ = x_sample.shape
    past = page_table.shape[1] * cache_k.shape[2]
    k_past = cache_k[:, page_table].reshape(cache_k.shape[0], bs, past, N_HEADS, HEAD_DIM)
    v_past = cache_v[:, page_table].reshape(cache_v.shape[0], bs, past, N_HEADS, HEAD_DIM)
    q_pos_s = past + jnp.arange(ts, dtype=jnp.int32)
    k_pos_s = jnp.arange(past + ts, dtype=jnp.int32)
    y_sample, new_conv_sample, new_ffn_sample, new_k_sample, new_v_sample = trunk(
        x_sample, q_pos_s, k_pos_s, state_conv, state_ffn, k_past, v_past,
        norm_mix, norm_ffn, norm_final, w_sc_in, w_sc_dw, w_sc_out,
        w_qkv, w_o, sb_bias, w_ffn_up, w_ffn_dw, b_ffn_dw, w_ffn_down)

    return (y_prompt, y_sample, new_k_prompt, new_v_prompt, new_conv_prompt, new_ffn_prompt,
            new_k_sample, new_v_sample, new_conv_sample, new_ffn_sample)


_drawn_inputs = setup_inputs


def setup_inputs(seed=0):
    import zlib

    import numpy as np

    out = dict(_drawn_inputs(seed))
    spreads = {}
    factors = {'norm_final': 8.123,
     'sb_bias': 29.728,
     'b_ffn_dw': 8.0,
     'cache_k': 8.0,
     'cache_v': 8.0,
     'w_o': 8.0}
    for name, (base, spread) in spreads.items():
        noise = np.random.default_rng([zlib.crc32(name.encode()), seed]).standard_normal(out[name].shape)
        drawn = base * np.exp(spread * noise) if base else spread * noise
        out[name] = __import__('jax').numpy.asarray(drawn.astype(out[name].dtype))
    for name, factor in factors.items():
        out[name] = (out[name] * factor).astype(out[name].dtype)
    return out
```

```python
import concourse.bass as bass
from concourse import mybir
from contextlib import ExitStack

P = 128
D = 1024
KC = D // P
SEQ = 1024
NB, NT = 8, 4
NS = NB * NT
T = SEQ + NS
TJ = 3
TW = T // TJ
F = 2816
FC = F // P
CW = 3
H, DH = 16, 64
PAGES, PG = 2, 128
PAST = PAGES * PG
EPS = 1e-6
MASKED = -1e30

N_SC_IN, N_SC_OUT, N_FFN, N_QKV, N_WO = 3 * KC, KC, 3 * FC, 3 * KC, KC
T_SC_IN = 0
T_SC_OUT = T_SC_IN + N_SC_IN
T_FFN0 = T_SC_OUT + N_SC_OUT
T_QKV = T_FFN0 + N_FFN
T_WO = T_QKV + N_QKV
T_FFN1 = T_WO + N_WO
N_TILES = T_FFN1 + N_FFN
RAW, SPLIT = 2, 3
UNROLL = RAW * SPLIT

PAIRS = FC // 2
FFN_TRIPS = (PAIRS - 1) // 2
FFN_OUT = 4 * PAIRS + KC * PAIRS
TRIP_FILLS = 4 + KC

FULL = {}
FREE = {}


def _count():
    full, free = [0, 0], [0, 0]

    def phase(name, full0, full1, free0=None, free1=None):
        FULL[name] = tuple(full)
        FREE[name] = tuple(free)
        full[0] += full0
        full[1] += full1
        free[0] += full0 if free0 is None else free0
        free[1] += full1 if free1 is None else free1

    phase("norm0", 1, 0)
    phase("sc_in", N_SC_IN // 2, N_SC_IN // 2)
    phase("sc_out", KC // 2, KC // 2)
    phase("norm1", 1, 0)
    phase("ffn0", FFN_OUT // 2, FFN_OUT // 2)
    phase("norm2", 1, 0)
    phase("qkv", 2 * KC, KC, 3 * KC, 2 * KC)
    phase("wo", KC // 2, KC // 2)
    phase("norm3", 1, 0)
    phase("ffn1", FFN_OUT // 2, FFN_OUT // 2)
    phase("norm4", 1, 0)


_count()
M_SC, M_FFN = 0, (KC, KC + FC)
H_SC_IN, H_SC_OUT, H_FFN0, H_QKV, H_WO, H_FFN1 = (KC * n for n in range(6))
STEPS = 2 * (SEQ // P)


def build(nc, x_in, weights, taps_sc, taps_ffn, state_sc, state_ffn, gains, bias_heads, bias_rows,
          cache_k, cache_v, pages, mask_diag, mask_new, ident_in, ident_b_in,
          y_out, k_out, v_out, conv_out, ffn_out):
    f32, f32r, bf16, i32 = mybir.dt.float32, mybir.dt.float32r, mybir.dt.bfloat16, mybir.dt.int32
    ACT, ALU = mybir.ActivationFunctionType, mybir.AluOpType
    ds = bass.ds
    ctx = ExitStack()
    with ctx:
        base = -(-nc.sbuf_base // 64) * 64
        arena = nc.sbuf_usable_end - base
        arena -= arena % 64
        ctx.enter_context(nc.sbuf_tensor("arena", [P, arena // 4], f32))
        top = [base]

        def at(offset, name, shape, dt):
            return nc.alloc_sbuf_tensor_at(name, shape, dt, offset=offset)

        def size(shape, dt):
            n = 1
            for d in shape[1:]:
                n *= d
            return -(-n * (2 if dt == bf16 else 4) // 32) * 32

        def sb(name, shape, dt=f32):
            t = at(top[0], name, shape, dt)
            top[0] += size(shape, dt)
            assert top[0] <= base + arena, name
            return t

        x = sb("x", [P, KC, T])
        h_at = top[0]
        h_hi = sb("h_hi", [P, KC, T], f32r)
        h_lo = sb("h_lo", [P, KC, T], f32r)
        h_end = top[0]
        raw = [sb(f"raw{n}", [P, D]) for n in range(RAW)]
        w_hi = [sb(f"w_hi{n}", [P, D], f32r) for n in range(SPLIT)]
        w_lo = [sb(f"w_lo{n}", [P, D], f32r) for n in range(SPLIT)]
        mean = sb("mean", [P, P])
        ident = sb("ident", [P, P])
        ident_b = sb("ident_b", [P, P], bf16)
        diag_b = sb("diag_b", [P, P], bf16)
        new_b = sb("new_b", [P, NB // 2, NS], bf16)
        gain = sb("gain", [P, 5, KC])
        tap_sc = sb("tap_sc", [P, KC, CW + 1])
        tap_ffn = sb("tap_ffn", [P, 2 * FC, CW + 1])
        st_sc = sb("st_sc", [P, KC, NB, CW - 1])
        st_ffn = sb("st_ffn", [P, 2 * FC, NB, CW - 1])
        new_sc = sb("new_sc", [P, KC, (1 + NB) * (CW - 1)])
        new_ffn = sb("new_ffn", [P, FC, (1 + NB) * (CW - 1)])
        bias_h = sb("bias_h", [P, 2, H])
        bias_r = sb("bias_r", [P, 2])
        eps = sb("eps", [P, 1])
        bias_now = [sb(f"bias_now{n}", [P, 1]) for n in range(2)]
        bias_pair = sb("bias_pair", [P, 2, 2])
        page_row = sb("page_row", [1, NB * PAGES], i32)
        overlay = top[0]
        mixed = sb("mixed", [P, KC, T])
        after_mixed = top[0]
        ext = [sb(f"ext{n}", [P, T + CW - 1]) for n in range(2)]
        smp = [sb(f"smp{n}", [P, NB, CW - 1 + NT]) for n in range(2)]
        y = [sb(f"y{n}", [P, T]) for n in range(2)]
        square = [sb(f"square{n}", [P, T]) for n in range(2)]
        total = sb("total", [P, T])
        hn = [square[0], square[1]]
        rstd = total
        c_gate = square
        top[0] = overlay
        a_hi = sb("a_hi", [P, 2, 2, T], f32r)
        a_lo = sb("a_lo", [P, 2, 2, T], f32r)
        assert top[0] == after_mixed
        q_t = sb("q_t", [P, T])
        k_t = sb("k_t", [P, T])
        v_t = sb("v_t", [P, T])
        keep = at(top[0] - size([P, T], f32), "keep", [P, SEQ], f32)
        v_rows = sb("v_rows", [P, SEQ // P, P])
        q_s = sb("q_s", [P, KC, NS])
        k_s = sb("k_s", [P, KC, NS])
        v_s = sb("v_s", [P, KC, NS])
        beta = [sb(f"beta{n}", [P, SEQ]) for n in range(2)]
        prod = sb("prod", [P, SEQ])
        w_t = [sb(f"w_t{n}", [P, 4, P]) for n in range(2)]
        top[0] = h_at
        page_k = [sb(f"page_k{n}", [P, KC, PAGES, PG]) for n in range(4)]
        page_v = [sb(f"page_v{n}", [P, PAGES, D]) for n in range(4)]
        assert top[0] <= h_end
        top[0] = after_mixed
        q_rows = sb("q_rows", [P, KC, P])
        v_new = sb("v_new", [NS, D])
        assert top[0] <= after_mixed + 3 * size([P, T], f32)
        top[0] = after_mixed + 3 * size([P, T], f32) + size(v_rows.shape, f32) + 3 * size(q_s.shape, f32)
        beta_s = sb("beta_s", [P, PAST + NS])
        keep_s = sb("keep_s", [P, PAST + NS])
        prod_s = sb("prod_s", [P, PAST + NS])
        w_ts = sb("w_ts", [P, PAGES + 1, P])

        bank = [ctx.enter_context(nc.psum_tensor(f"bank{n}", [P, 3 if n < 2 else 2, 512], f32)) for n in range(3)]
        out = [bank[0], bank[1]]
        spare = bank[2]

        def result(s):
            return out[s][:, :, 0:TW]

        score = [out[1][:, 0:2, :].rearrange("p a b -> p (a b)"), spare[:, :, :].rearrange("p a b -> p (a b)")]
        turned = [out[1][:, 2, :], out[0][:, 2, :]]
        attended = out[0][:, 0:2, :].rearrange("p a b -> p (a b)")

        def sem(name):
            return ctx.enter_context(nc.semaphore(name))

        raw_loaded = [sem(f"raw_loaded{n}") for n in range(RAW)]
        w_high = sem("w_high")
        w_split = sem("w_split")
        w_used = sem("w_used")
        full = [sem("full0"), sem("full1")]
        taken = [sem("taken0"), sem("taken1")]
        x_loaded = sem("x_loaded")
        consts = sem("consts")
        state_loaded = sem("state_loaded")
        made = sem("made")
        negated = sem("negated")
        rstd_made = sem("rstd_made")
        bias_set = sem("bias_set")
        pair_bias_set = sem("pair_bias_set")
        split_begun = sem("split_begun")
        new_copied = sem("new_copied")
        squared = sem("squared")
        summed = sem("summed")
        normed = sem("normed")
        h_high = sem("h_high")
        h_ready = sem("h_ready")
        smp_full = sem("smp_full")
        tapped = sem("tapped")
        convolved = sem("convolved")
        silued = sem("silued")
        a_high = sem("a_high")
        a_ready = sem("a_ready")
        kv_stored = sem("kv_stored")
        v_turned = sem("v_turned")
        v_ready = sem("v_ready")
        scored = sem("scored")
        beta_done = sem("beta_done")
        keep_done = sem("keep_done")
        scanned = sem("scanned")
        weighed = sem("weighed")
        turn_done = sem("turn_done")
        w_t_ready = sem("w_t_ready")
        pv_done = sem("pv_done")
        page_in = [sem(f"page_in{n}") for n in range(4)]
        page_ids = sem("page_ids")
        s_set = sem("s_set")
        s_scored = sem("s_scored")
        s_beta = sem("s_beta")
        s_keep = sem("s_keep")
        s_scan = sem("s_scan")
        s_weighed = sem("s_weighed")
        s_turned = sem("s_turned")
        s_wt = sem("s_wt")
        s_full = sem("s_full")
        s_vturned = sem("s_vturned")
        s_vnew = sem("s_vnew")
        s_out = sem("s_out")
        y_made = sem("y_made")
        stored = sem("stored")

        block = ctx.enter_context(nc.Block())

        units = []
        for j in range(STEPS):
            blocks = j // 2 + 1
            for first in range(0, blocks, 4):
                units.append((j, first, min(4, blocks - first)))
        UNITS = len(units)

        @block.sync
        def _(sp):
            def load_tile(n, slot):
                sp.wait_ge(w_split, n + 1)
                sp.dma_start(raw[slot][:, :], weights[ds(n, 1), :, :].rearrange("o p n -> p (o n)")).then_inc(raw_loaded[slot], 16)

            sp.sem_inc(w_split, RAW)
            sp.sem_inc(s_full, 2)
            sp.dma_start(page_row[:, :], pages).then_inc(page_ids, 16)
            sp.wait_ge(page_ids, 16)
            early = T_WO + SPLIT + 1
            assert early % UNROLL == 0
            with sp.Fori(0, early // UNROLL) as i:
                for u in range(UNROLL):
                    load_tile(i * UNROLL + u, u % RAW)
            sp.wait_ge(taken[0], FREE["qkv"][0] + 3 * (KC - 1) + 2 + 1)
            with sp.Fori(0, 2) as i:
                for n in range(4):
                    sp.wait_ge(s_full, i * 2 + (n // 2 + 1))
                    for g in range(PAGES):
                        page = sp.value_load(page_row[0:1, ds(i * 8 + n * PAGES + g, 1)],
                                             min_val=0, max_val=cache_k.shape[0] - 1)
                        sp.dma_start(page_k[n][:, :, g, :], cache_k[ds(page, 1), :, :, :].rearrange("o p c t -> p (o c) t")).then_inc(page_in[n], 16)
                        sp.dma_start(page_v[n][:, g, :], cache_v[ds(page, 1), :, :].rearrange("o p n -> p (o n)")).then_inc(page_in[n], 16)
            rest = N_TILES - early
            with sp.Fori(0, rest // UNROLL) as i:
                for u in range(UNROLL):
                    load_tile(i * UNROLL + (early + u), u % RAW)
            for n in range(rest - rest % UNROLL, rest):
                load_tile(early + n, n % RAW)

        @block.gpsimd
        def _(pool):
            def split_tile(n, slot, ring, nth):
                pool.wait_ge(raw_loaded[slot], nth * 16)
                pool.wait_ge(w_used, n + 1)
                pool.sem_inc(split_begun, 1)
                nc.gpsimd.tensor_copy(w_hi[ring][:, :], raw[slot][:, :]).then_inc(w_high, 1)
                pool.wait_ge(w_high, n + 1)
                nc.gpsimd.tensor_tensor(w_lo[ring][:, :], raw[slot][:, :], w_hi[ring][:, :].bitcast(f32),
                                        ALU.subtract).then_inc(w_split, 1)

            pool.sem_inc(w_used, SPLIT - 1)
            with pool.Fori(0, N_TILES // UNROLL) as i:
                for u in range(UNROLL):
                    split_tile(i * UNROLL + u, u % RAW, u % SPLIT, i * (UNROLL // RAW) + (u // RAW + 1))
            for n in range(N_TILES - N_TILES % UNROLL, N_TILES):
                split_tile(n, n % RAW, n % SPLIT, n // RAW + 1)

        @block.tensor
        def _(pe):
            def three(o, w, c0, hi, lo, first, last, counts=False):
                mm = nc.tensor.matmul(o, w_hi[w][:, c0:c0 + P], hi, start=first, stop=False)
                if counts:
                    mm.then_inc(w_used, 1)
                nc.tensor.matmul(o, w_hi[w][:, c0:c0 + P], lo, start=False, stop=False)
                return nc.tensor.matmul(o, w_lo[w][:, c0:c0 + P], hi, start=False, stop=last)

            def norm_sum(name, nth):
                pe.wait_ge(summed, KC * (nth + 1))
                pe.wait_ge(taken[0], FREE[name][0] + 1)
                for j in range(TJ):
                    mm = nc.tensor.matmul(out[0][:, j, 0:TW], mean[:, :], total[:, j * TW:(j + 1) * TW],
                                          start=True, stop=True)
                mm.then_inc(full[0], 1)

            def linear(tile, ring, s, fill, h_base=None):
                pe.wait_ge(w_split, tile + (RAW + 1))
                pe.wait_ge(taken[s], fill + 1)
                for k in range(KC):
                    if h_base is not None:
                        pe.wait_ge(h_ready, h_base + k + 1)
                    for j in range(TJ):
                        mm = three(out[s][:, j, 0:TW], ring, k * P, h_hi[:, k, j * TW:(j + 1) * TW],
                                   h_lo[:, k, j * TW:(j + 1) * TW], k == 0, k == KC - 1,
                                   k == j == 0)
                mm.then_inc(full[s], 1)

            def tiles_of(name, tile0, h_base):
                for k in range(KC):
                    s = (k + 1) % 2
                    linear(tile0 + k, (tile0 + k) % SPLIT, s, FREE[name][s] + k // 2,
                           h_base if k == 0 else None)

            def up(tile, ring0, k0, name, trip, h_base=None):
                for n in range(4):
                    s = (k0 + n + 1) % 2
                    linear(tile + n, (ring0 + n) % SPLIT, s, trip * TRIP_FILLS + (FREE[name][s] + (k0 + n) // 2),
                           h_base if n == 0 else None)

            def down(tile, ring0, k0, name, trip, slot, group):
                pe.wait_ge(w_split, tile + (RAW + 2))
                pe.wait_ge(a_ready, group * 2 + 4)
                for f in range(KC):
                    s = (k0 + f + 1) % 2
                    pe.wait_ge(taken[s], trip * TRIP_FILLS + (FREE[name][s] + (k0 + f) // 2 + 1))
                    for kk in range(2):
                        for j in range(TJ):
                            mm = three(out[s][:, j, 0:TW], (ring0 + kk) % SPLIT, f * P,
                                       a_hi[:, slot, kk, j * TW:(j + 1) * TW],
                                       a_lo[:, slot, kk, j * TW:(j + 1) * TW], kk == 0, kk == 1,
                                       j == 0 and (f, kk) in ((0, 0), (KC - 1, 1)))
                    mm.then_inc(full[s], 1)

            def ffn(layer):
                name = f"ffn{layer}"
                t0 = (T_FFN0, T_FFN1)[layer]
                g0 = layer * PAIRS
                up(t0, t0, 0, name, 0, (H_FFN0, H_FFN1)[layer])
                with pe.Fori(0, FFN_TRIPS) as i:
                    for n in range(2):
                        r0 = t0 + 4 + 6 * n
                        k0 = 4 + (4 + KC) * n
                        up(i * 12 + r0, r0, k0, name, i)
                        down(i * 12 + (r0 + 4), r0 + 4, k0 + 4, name, i, n, i * 2 + (g0 + n))
                last = 4 + 6 * (PAIRS - 1)
                down(t0 + last, t0 + last, 4 + (4 + KC) * (PAIRS - 1), name, 0, 0, g0 + PAIRS - 1)

            pe.wait_ge(made, 1)
            norm_sum("norm0", 0)
            with pe.Fori(0, KC // 2) as i:
                for n in range(6):
                    s = (n + 1) % 2
                    linear(i * 6 + n, n % SPLIT, s, i * 3 + (FREE["sc_in"][s] + n // 2), H_SC_IN if n == 0 else None)
            tiles_of("sc_out", T_SC_OUT, H_SC_OUT)
            norm_sum("norm1", 1)
            ffn(0)
            norm_sum("norm2", 2)

            def scores(pair, j):
                i, h = divmod(j, 2)
                rows = slice(DH * h, DH * h + DH)
                pe.wait_ge(keep_done, pair * STEPS + (j - 2 + 1 + 2))
                width = P * (i + 1)
                for n0 in range(0, width, 512):
                    n1 = min(n0 + 512, width)
                    nc.tensor.matmul(score[j % 2][:, n0:n1], q_t[rows, i * P:(i + 1) * P], k_t[rows, n0:n1],
                                     start=True, stop=n1 < width)
                nc.tensor.matmul(score[j % 2][:, width - P:width], ident_b[:, :], diag_b[:, :],
                                 start=False, stop=True).then_inc(scored, 1)

            def turn(pair, u):
                j, first, n = units[u]
                pe.wait_ge(weighed, pair * STEPS + (j + 2))
                pe.wait_ge(w_t_ready, pair * UNITS + (u - 2 + 1 + 2))
                for b in range(n):
                    mm = nc.tensor.transpose(turned[u % 2][:, b * P:(b + 1) * P],
                                             beta[j % 2][:, (first + b) * P:(first + b + 1) * P], ident[:, :])
                mm.then_inc(turn_done, 1)

            def values(pair, u):
                j, first, n = units[u]
                i, h = divmod(j, 2)
                pe.wait_ge(w_t_ready, pair * UNITS + (u + 1 + 2))
                for b in range(n):
                    mm = nc.tensor.matmul(attended[DH * h:DH * h + DH, i * P:(i + 1) * P],
                                          v_rows[:, first + b, DH * h:DH * h + DH], w_t[u % 2][:, b, :],
                                          start=first + b == 0, stop=first + b == i)
                mm.then_inc(pv_done, 1)

            with pe.Fori(0, KC) as c:
                tile = c * 3 + T_QKV
                f0 = c * 3 + FREE["qkv"][0]
                f1 = c * 2 + FREE["qkv"][1]
                linear(tile, T_QKV % SPLIT, 0, f0, H_QKV)
                linear(tile + 1, (T_QKV + 1) % SPLIT, 1, f1)
                pe.wait_ge(taken[0], f0 + 2)
                pe.wait_ge(keep_done, c * STEPS + 2)
                for b in range(SEQ // P):
                    mm = nc.tensor.transpose(score[1][:, b * P:(b + 1) * P], v_t[:, b * P:(b + 1) * P], ident[:, :])
                mm.then_inc(v_turned, 1)
                linear(tile + 2, (T_QKV + 2) % SPLIT, 0, f0 + 1)
                pe.wait_ge(v_ready, c + 1)
                pe.wait_ge(taken[0], f0 + 3)
                pe.wait_ge(taken[1], f1 + 2)
                scores(c, 0)
                scores(c, 1)
                turn(c, 0)
                scores(c, 2)
                for u in range(UNITS):
                    if u + 1 < UNITS:
                        turn(c, u + 1)
                        j, first, _ = units[u + 1]
                        if first == 0 and j + 2 < STEPS:
                            scores(c, j + 2)
                    values(c, u)

            pe.wait_ge(taken[0], FREE["wo"][0] + 1)
            pe.wait_ge(taken[1], FREE["wo"][1] + 1)
            for c in range(KC):
                mm = nc.tensor.transpose(score[1][0:NS, c * P:(c + 1) * P], v_s[:, c, :], ident[:, :])
            mm.then_inc(s_vturned, 1)
            with pe.Fori(0, 2) as i:
                for n in range(2):
                    bp = i * 2 + n
                    pe.wait_ge(s_set, bp + 1)
                    for b in range(2):
                        rows = slice(64 * b, 64 * b + 64)
                        pe.wait_ge(page_in[2 * n + b], i * 64 + 64)
                        for part in range(2):
                            for c in range(KC):
                                keys = page_k[2 * n + b][:, c, :, :] if part == 0 else k_s[:, c, :]
                                o = out[1][rows, part, 0:PAST if part == 0 else NS]
                                nc.tensor.matmul(o, q_rows[:, c, rows], keys, start=c == 0,
                                                 stop=c == KC - 1, skip_group_check=True)
                    nc.tensor.matmul(out[1][:, 1, 0:NS], ident_b[:, :], new_b[:, ds(bp, 1), :].rearrange("p o t -> p (o t)"), start=False,
                                     stop=True, skip_group_check=True).then_inc(s_scored, 1)
                    pe.wait_ge(s_weighed, bp + 1)
                    for g in range(PAGES):
                        nc.tensor.transpose(out[1][:, 2, g * P:(g + 1) * P], beta_s[:, g * P:(g + 1) * P], ident[:, :])
                    nc.tensor.transpose(out[1][0:NS, 2, PAST:PAST + P], beta_s[:, PAST:PAST + NS],
                                        ident[:, :]).then_inc(s_turned, 1)
                    pe.wait_ge(s_wt, bp + 1)
                    pe.wait_ge(s_vnew, 1)
                    pe.wait_ge(s_out, bp + 1)
                    for b in range(2):
                        for c in range(KC):
                            o = out[0][:, 2, (b * KC + c) * 8:(b * KC + c + 1) * 8]
                            cols = slice(64 * b + 8 * c, 64 * b + 8 * c + 8)
                            for g in range(PAGES):
                                nc.tensor.matmul(o, page_v[2 * n + b][:, g, c * P:(c + 1) * P], w_ts[:, g, cols],
                                                 start=g == 0, stop=False)
                            mm = nc.tensor.matmul(o, v_new[:, c * P:(c + 1) * P], w_ts[0:NS, PAGES, cols],
                                                  start=False, stop=True)
                    mm.then_inc(s_full, 1)

            pe.wait_ge(s_out, NB // 2 + 1)
            tiles_of("wo", T_WO, H_WO)
            norm_sum("norm3", 3)
            ffn(1)
            norm_sum("norm4", 4)

        @block.scalar
        def _(act):
            def act_op(o, i, func=ACT.Copy, **kw):
                return nc.scalar.activation(o, i, func, **kw)

            for f in range(KC):
                act.dma_start(x[:, f, :], x_in[f, :, :]).then_inc(x_loaded, 16)
            act.dma_start(gain[:, :, :], gains).then_inc(consts, 16)
            act.dma_start(tap_sc[:, :, :], taps_sc).then_inc(consts, 16)
            act.dma_start(tap_ffn[:, :, :], taps_ffn).then_inc(consts, 16)
            act.dma_start(ident[:, :], ident_in).then_inc(consts, 16)
            act.dma_start(ident_b[:, :], ident_b_in).then_inc(consts, 16)
            act.dma_start(diag_b[:, :], mask_diag).then_inc(consts, 16)
            act.dma_start(new_b[:, :, :], mask_new).then_inc(consts, 16)
            act.dma_start(bias_h[:, 0, :], bias_heads).then_inc(consts, 16)
            act.dma_start(bias_r[:, 0:1], bias_rows).then_inc(consts, 16)
            act.dma_start(st_sc[:, :, :, :], state_sc).then_inc(state_loaded, 16)
            act.dma_start(st_ffn[:, :, :, :], state_ffn).then_inc(state_loaded, 16)
            act.sem_inc(convolved, 2)

            def norm(nth, layer_before, k_before, keep_h=True):
                for f in range(KC):
                    if nth == 0 and f == 0:
                        act.wait_ge(x_loaded, 16 * KC)
                    elif nth:
                        k = k_before + f
                        s = (k + 1) % 2
                        act.wait_ge(taken[s], FREE[layer_before][s] + k // 2 + 2)
                    if f >= 2:
                        act.wait_ge(summed, KC * nth + f - 1)
                    act_op(square[f % 2][:, :], x[:, f, :], ACT.Square).then_inc(squared, 1)
                act.wait_ge(full[0], FULL[f"norm{nth}"][0] + 1)
                act_op(total[:, :].rearrange("p (a b) -> p a b", a=TJ), result(0), ACT.Sqrt,
                       bias=eps[:, 0:1]).then_inc(taken[0], 1)
                if keep_h:
                    for f in range(KC):
                        act.wait_ge(normed, KC * nth + f + 1)
                        act_op(h_hi[:, f, :], hn[f % 2][:, :]).then_inc(h_high, 1)

            def split_mixed():
                for f in range(KC):
                    act_op(h_hi[:, f, :], mixed[:, f, :]).then_inc(h_high, 1)

            def samples(m, par, states, kept):
                tokens = ext[par][:, CW - 1 + SEQ:CW - 1 + T].rearrange("p (b t) -> p b t", t=NT)
                act_op(smp[par][:, :, CW - 1:], tokens).then_inc(smp_full, 1)
                act_op(smp[par][:, :, 0:CW - 1], states).then_inc(smp_full, 1)
                act_op(kept[:, 0:CW - 1], ext[par][:, SEQ:SEQ + CW - 1]).then_inc(smp_full, 1)
                act_op(kept[:, CW - 1:].rearrange("p (b t) -> p b t", t=CW - 1),
                       tokens[:, :, NT - CW + 1:]).then_inc(smp_full, 1)

            def ffn_chunk(m, par, chunk, layer, k, trip, slot, group):
                name = f"ffn{layer}"
                s = (k + 1) % 2
                gate = trip * TRIP_FILLS + (FULL[name][s] + k // 2 + 1)
                gate_taken = trip * TRIP_FILLS + (FREE[name][s] + k // 2 + 2)
                act.wait_ge(convolved, m + 1)
                act.wait_ge(full[s], gate)
                act_op(ext[par][:, CW - 1:].rearrange("p (a b) -> p a b", a=TJ), result(s)).then_inc(taken[s], 1)
                act.wait_ge(taken[s], gate_taken)
                samples(m, par, st_ffn[:, ds(chunk + layer * FC, 1), :, :].rearrange("p o b t -> p (o b) t"),
                        new_ffn[:, ds(chunk, 1), :].rearrange("p o t -> p (o t)"))
                act_op(bias_now[par][:, :], tap_ffn[:, ds(chunk + layer * FC, 1), CW:CW + 1].rearrange("p o t -> p (o t)")
                       ).then_inc(bias_set, 1)
                act.wait_ge(bias_set, m - (KC - 1))
                act.wait_ge(convolved, m + 3)
                act_op(y[par][:, :], y[par][:, :], ACT.Silu, bias=bias_now[par][:, :]).then_inc(silued, 1)
                s = (k + 2) % 2
                act.wait_ge(taken[s], trip * TRIP_FILLS + (FREE[name][s] + (k + 1) // 2 + 2))
                if par == 0 and group is not None:
                    act.wait_ge(taken[0], group)
                act_op(a_hi[:, slot, par, :], y[par][:, :]).then_inc(a_high, 1)

            def ffn(layer):
                name = f"ffn{layer}"
                m0 = M_FFN[layer]
                for p in range(2):
                    ffn_chunk(m0 + p, p, p, layer, 2 * p, 0, 0, None)
                with act.Fori(0, FFN_TRIPS) as i:
                    for n in range(2):
                        k0 = (4 + KC) * n + 4
                        for p in range(2):
                            ffn_chunk(i * 4 + (m0 + 2 + 2 * n + p), p, i * 4 + (2 + 2 * n + p), layer,
                                      k0 + 2 * p, i, (n + 1) % 2, i * TRIP_FILLS + (FREE[name][0] + (k0 - 1) // 2 + 2))
                act.wait_ge(smp_full, 4 * (m0 + FC))
                act.dma_start(ffn_out[layer], new_ffn[:, :, :]).then_inc(stored, 16)

            act.wait_ge(consts, 16 * 9)
            act_op(bias_h[:, 1, :], bias_h[:, 0, :], scale=-1.0).then_inc(negated, 1)
            act_op(bias_r[:, 1:2], bias_r[:, 0:1], scale=-1.0).then_inc(negated, 1)
            act.wait_ge(made, 2)
            norm(0, None, 0)
            act.wait_ge(state_loaded, 32)
            act.wait_ge(h_ready, KC)
            with act.Fori(0, KC // 2) as i:
                for n in range(2):
                    k = 3 * n
                    s = (k + 1) % 2
                    m = i * 2 + n
                    act.wait_ge(convolved, m + 1)
                    act.wait_ge(full[s], i * 3 + (FULL["sc_in"][s] + k // 2 + 1))
                    act_op(c_gate[n][:, :].rearrange("p (a b) -> p a b", a=TJ), result(s)).then_inc(taken[s], 1)
                    s = (k + 2) % 2
                    act.wait_ge(taken[s], i * 3 + (FREE["sc_in"][s] + (k + 1) // 2 + 2))
                    samples(m, n, st_sc[:, ds(m, 1), :, :].rearrange("p o b t -> p (o b) t"),
                            new_sc[:, ds(m, 1), :].rearrange("p o t -> p (o t)"))
            act.wait_ge(smp_full, 4 * KC)
            act.dma_start(conv_out, new_sc[:, :, :]).then_inc(stored, 16)
            act.wait_ge(taken[0], FREE["sc_out"][0] + 1)
            split_mixed()
            norm(1, "sc_out", 0)
            ffn(0)
            norm(2, "ffn0", FFN_OUT - KC)

            act.wait_ge(negated, 2)
            with act.Fori(0, KC) as c:
                def take(dst, s, nth, **kw):
                    act.wait_ge(full[s], nth[0] + 1)
                    act_op(dst[:, :].rearrange("p (a b) -> p a b", a=TJ), result(s), **kw).then_inc(taken[s], 1)
                    act.wait_ge(taken[s], nth[1] + 2)

                def new_tokens(dst, src):
                    act_op(dst[:, ds(c, 1), :].rearrange("p o t -> p (o t)"), src[:, SEQ:T]).then_inc(new_copied, 1)

                act.wait_ge(scanned, c * STEPS + 1)
                take(v_t, 0, (c * 2 + FULL["qkv"][0], c * 3 + FREE["qkv"][0]))
                act.dma_start(v_out[ds(c, 1), :, :].rearrange("o p t -> p (o t)"), v_t[:, :]).then_inc(kv_stored, 16)
                new_tokens(v_s, v_t)
                take(q_t, 1, (c + FULL["qkv"][1], c * 2 + FREE["qkv"][1]), scale=DH ** -0.5)
                act.wait_ge(v_turned, c + 1)
                act_op(v_rows[:, :, :].rearrange("p a b -> p (a b)"), score[1][:, :]).then_inc(v_ready, 1)
                new_tokens(q_s, q_t)
                act_op(bias_pair[:, :, :], bias_h[:, :, ds(c * 2, 2)]).then_inc(pair_bias_set, 1)
                take(k_t, 0, (c * 2 + (FULL["qkv"][0] + 1), c * 3 + (FREE["qkv"][0] + 1)))
                act.dma_start(k_out[ds(c, 1), :, :].rearrange("o p t -> p (o t)"), k_t[:, :]).then_inc(kv_stored, 16)
                new_tokens(k_s, k_t)
                act.wait_ge(new_copied, c * 3 + 3)
                act.wait_ge(pair_bias_set, c + 1)
                act.wait_ge(kv_stored, c * 32 + 32)
                for j in range(STEPS):
                    i, h = divmod(j, 2)
                    width = P * (i + 1)
                    act.wait_ge(scored, c * STEPS + (j + 1))
                    if j >= 2:
                        turns = sum(unit[0] <= j - 2 for unit in units)
                        act.wait_ge(turn_done, c * UNITS + turns)
                    act_op(beta[j % 2][:, 0:width], score[j % 2][:, 0:width], ACT.Sigmoid,
                           bias=bias_pair[:, 0, h:h + 1]).then_inc(beta_done, 1)
                    act.wait_ge(scanned, c * STEPS + (j + 1))
                    act_op(keep[:, 0:width], score[j % 2][:, 0:width], ACT.Sigmoid, scale=-1.0,
                           bias=bias_pair[:, 1, h:h + 1]).then_inc(keep_done, 1)
            with act.Fori(0, 4) as bp:
                act.wait_ge(s_scored, bp + 1)
                for part, (n0, n1) in enumerate(((0, PAST), (PAST, PAST + NS))):
                    act_op(beta_s[:, n0:n1], out[1][:, part, 0:n1 - n0], ACT.Sigmoid, bias=bias_r[:, 0:1]).then_inc(s_beta, 1)
                    act_op(keep_s[:, n0:n1], out[1][:, part, 0:n1 - n0], ACT.Sigmoid, scale=-1.0,
                           bias=bias_r[:, 1:2]).then_inc(s_keep, 1)
            act.wait_ge(s_out, NB // 2 + 1)
            split_mixed()
            norm(3, "wo", 0)
            ffn(1)
            norm(4, "ffn1", FFN_OUT - KC, keep_h=False)
            for f in range(KC):
                act.wait_ge(y_made, f + 1)
                act.dma_start(y_out[f, :, :], x[:, f, :]).then_inc(stored, 16)
            act.wait_ge(stored, 16 * (3 + KC))
            act.wait_ge(kv_stored, 32 * KC)

        @block.vector
        def _(dve):
            V = nc.vector

            for s in range(2):
                dve.sem_inc(taken[s], 1)
            dve.sem_inc(scanned, 1)
            dve.sem_inc(keep_done, 2)
            dve.sem_inc(w_t_ready, 2)
            dve.sem_inc(s_out, 1)
            dve.sem_inc(a_ready, 2)
            dve.sem_inc(weighed, 1)
            V.memset(mean[:, :], 1.0 / D).then_inc(made, 1)
            V.memset(eps[:, :], EPS).then_inc(made, 1)
            for n in range(2):
                V.memset(ext[n][:, 0:CW - 1], 0.0).then_inc(made, 1)

            def norm(name, nth):
                for f in range(KC):
                    n = KC * nth + f
                    dve.wait_ge(squared, n + 1)
                    if f == 0:
                        V.tensor_copy(total[:, :], square[0][:, :]).then_inc(summed, 1)
                    else:
                        dve.wait_ge(summed, n)
                        V.tensor_tensor(total[:, :], total[:, :], square[f % 2][:, :], ALU.add).then_inc(summed, 1)
                dve.wait_ge(taken[0], FREE[name][0] + 2)
                V.reciprocal(rstd[:, :], total[:, :]).then_inc(rstd_made, 1)
                dve.wait_ge(rstd_made, nth + 1)

                def scaled(f, o):
                    return V.scalar_tensor_tensor(o, x[:, f, :], gain[:, nth, f:f + 1], rstd[:, :], ALU.mult, ALU.mult)

                if nth == 4:
                    for f in range(KC):
                        scaled(f, x[:, f, :]).then_inc(y_made, 1)
                    return

                def low(f):
                    dve.wait_ge(h_high, H_BASE[nth] + f + 1)
                    V.tensor_tensor(h_lo[:, f, :], hn[f % 2][:, :], h_hi[:, f, :].bitcast(f32),
                                    ALU.subtract).then_inc(h_ready, 1)

                for f in range(KC):
                    if f >= 2:
                        dve.wait_ge(h_ready, H_BASE[nth] + f - 1)
                    scaled(f, hn[f % 2][:, :]).then_inc(normed, 1)
                    if f >= 1:
                        low(f - 1)
                low(KC - 1)

            H_BASE = {0: H_SC_IN, 1: H_FFN0, 2: H_QKV, 3: H_FFN1}

            def split_mixed(h_base):
                for f in range(KC):
                    dve.wait_ge(h_high, h_base + f + 1)
                    V.tensor_tensor(h_lo[:, f, :], mixed[:, f, :], h_hi[:, f, :].bitcast(f32),
                                    ALU.subtract).then_inc(h_ready, 1)

            def conv(m, par, tap):
                e, o = ext[par], y[par]
                V.tensor_scalar(o[:, 0:SEQ], e[:, 0:SEQ], tap(0), None, ALU.mult).then_inc(tapped, 1)
                dve.wait_ge(smp_full, m * 4 + 2)
                q, r = smp[par], y[par][:, SEQ:T].rearrange("p (b t) -> p b t", t=NT)
                V.tensor_scalar(r, q[:, :, 0:NT], tap(0), None, ALU.mult).then_inc(tapped, 1)
                for n in range(1, CW):
                    dve.wait_ge(tapped, m * 4 + (2 * n - 1))
                    main = V.scalar_tensor_tensor(o[:, 0:SEQ], e[:, n:n + SEQ], tap(n), o[:, 0:SEQ], ALU.mult, ALU.add)
                    if n < CW - 1:
                        main.then_inc(tapped, 1)
                    dve.wait_ge(tapped, m * 4 + 2 * n)
                    if n == CW - 1:
                        dve.wait_ge(smp_full, m * 4 + 4)
                    last = V.scalar_tensor_tensor(r, q[:, :, n:n + NT], tap(n), r, ALU.mult, ALU.add)
                    if n < CW - 1:
                        last.then_inc(tapped, 1)
                last.then_inc(convolved, 1)

            def ffn_chunk(m, par, chunk, layer, k, trip, slot):
                name = f"ffn{layer}"
                s = (k + 1) % 2
                dve.wait_ge(a_ready, m - (KC - 1))
                dve.wait_ge(taken[s], trip * TRIP_FILLS + (FREE[name][s] + k // 2 + 2))
                conv(m, par, lambda t: tap_ffn[:, ds(chunk + layer * FC, 1), t:t + 1].rearrange("p o t -> p (o t)"))
                s = (k + 2) % 2
                dve.wait_ge(silued, m - (KC - 1))
                dve.wait_ge(full[s], trip * TRIP_FILLS + (FULL[name][s] + (k + 1) // 2 + 1))
                yy = y[par][:, :].rearrange("p (a b) -> p a b", a=TJ)
                V.tensor_tensor(yy, yy, result(s), ALU.mult).then_inc(taken[s], 1)
                dve.wait_ge(a_high, m - (KC - 1))
                V.tensor_tensor(a_lo[:, slot, par, :], y[par][:, :], a_hi[:, slot, par, :].bitcast(f32),
                                ALU.subtract).then_inc(a_ready, 1)

            def add_x(f, name, k, trip):
                s = (k + 1) % 2
                dve.wait_ge(full[s], trip * TRIP_FILLS + (FULL[name][s] + k // 2 + 1))
                xx = x[:, f, :].rearrange("p (a b) -> p a b", a=TJ)
                V.tensor_tensor(xx, xx, result(s), ALU.add).then_inc(taken[s], 1)

            def ffn(layer):
                name = f"ffn{layer}"
                m0 = M_FFN[layer]

                def up(m, chunk, k0, trip, slot):
                    for p in range(2):
                        ffn_chunk(m + p, p, chunk + p, layer, k0 + 2 * p, trip, slot)

                def down(k0, trip):
                    for f in range(KC):
                        add_x(f, name, k0 + f, trip)

                up(m0, 0, 0, 0, 0)
                with dve.Fori(0, FFN_TRIPS) as i:
                    for n in range(2):
                        k0 = (4 + KC) * n + 4
                        up(i * 4 + (m0 + 2 + 2 * n), i * 4 + (2 + 2 * n), k0, i, (n + 1) % 2)
                        down(k0 + 4, i)
                down(FFN_OUT - KC, 0)

            dve.wait_ge(x_loaded, 16 * KC)
            dve.wait_ge(consts, 16 * 9)
            dve.wait_ge(made, 4)
            norm("norm0", 0)
            with dve.Fori(0, KC // 2) as i:
                for n in range(2):
                    m = i * 2 + n
                    k = 3 * n + 1
                    s = (k + 1) % 2
                    dve.wait_ge(convolved, m + 1)
                    gate = (k + 2) % 2
                    dve.wait_ge(taken[gate], i * 3 + (FREE["sc_in"][gate] + (k - 1) // 2 + 2))
                    dve.wait_ge(full[s], i * 3 + (FULL["sc_in"][s] + k // 2 + 1))
                    V.tensor_tensor(ext[n][:, CW - 1:].rearrange("p (a b) -> p a b", a=TJ),
                                    c_gate[n][:, :].rearrange("p (a b) -> p a b", a=TJ), result(s),
                                    ALU.mult).then_inc(taken[s], 1)
                    dve.wait_ge(taken[s], i * 3 + (FREE["sc_in"][s] + k // 2 + 2))
                    conv(m, n, lambda t: tap_sc[:, ds(m, 1), t:t + 1].rearrange("p o t -> p (o t)"))
                    k = 3 * n + 2
                    s = (k + 1) % 2
                    dve.wait_ge(convolved, m + 3)
                    dve.wait_ge(full[s], i * 3 + (FULL["sc_in"][s] + k // 2 + 1))
                    V.tensor_tensor(mixed[:, ds(m, 1), :].rearrange("p o (a b) -> p (o a) b", a=TJ),
                                    y[n][:, :].rearrange("p (a b) -> p a b", a=TJ), result(s),
                                    ALU.mult).then_inc(taken[s], 1)
            split_mixed(H_SC_OUT)
            for f in range(KC):
                add_x(f, "sc_out", f, 0)
            norm("norm1", 1)
            ffn(0)
            norm("norm2", 2)

            with dve.Fori(0, KC) as c:
                def copy_turned(u):
                    dve.wait_ge(turn_done, c * UNITS + (u + 1))
                    if u >= 2:
                        dve.wait_ge(pv_done, c * UNITS + (u - 1))
                    n = units[u][2]
                    V.tensor_copy(w_t[u % 2][:, 0:n, :].rearrange("p a b -> p (a b)"),
                                  turned[u % 2][:, 0:n * P]).then_inc(w_t_ready, 1)

                def weigh(j):
                    i = j // 2
                    width = P * (i + 1)
                    dve.wait_ge(beta_done, c * STEPS + (j + 1))
                    dve.wait_ge(keep_done, c * STEPS + (j + 1 + 2))
                    dve.wait_ge(weighed, c * STEPS + (j + 1))
                    V.tensor_tensor_scan(prod[:, width - 1:0:-1],
                                         keep[:, width - 1:0:-1], keep[:, width - 1:0:-1], 1.0,
                                         ALU.mult, ALU.bypass).then_inc(scanned, 1)
                    dve.wait_ge(scanned, c * STEPS + (j + 1 + 1))
                    V.tensor_tensor(beta[j % 2][:, 0:width - 1], beta[j % 2][:, 0:width - 1], prod[:, 1:width],
                                    ALU.mult).then_inc(weighed, 1)

                weigh(0)
                weigh(1)
                copy_turned(0)
                for u in range(UNITS):
                    if u + 1 < UNITS:
                        copy_turned(u + 1)
                        j, first, _ = units[u + 1]
                        if first == 0 and j + 1 < STEPS:
                            weigh(j + 1)
                dve.wait_ge(pv_done, c * UNITS + UNITS)
                for s in (1, 0):
                    half = slice((1 - s) * (SEQ // 2), (2 - s) * (SEQ // 2))
                    V.tensor_copy(mixed[:, ds(c, 1), half].rearrange("p o t -> p (o t)"),
                                  attended[:, half]).then_inc(taken[s], 1)

            V.memset(q_rows[:, :, :], 0.0).then_inc(made, 1)
            dve.wait_ge(made, 5)
            dve.wait_ge(s_vturned, 1)
            V.tensor_copy(v_new[:, :], score[1][0:NS, :]).then_inc(s_vnew, 1)
            with dve.Fori(0, 4) as bp:
                for c in range(KC):
                    for h in range(2):
                        rows = slice(DH * h, DH * h + DH)
                        col = (2 * c + h) * NT
                        o = q_rows[rows, c, :].rearrange("p (b r) -> p b r", b=2)[:, :, col:col + NT]
                        last = V.tensor_copy(o, q_s[rows, c, ds(bp * (2 * NT), 2 * NT)].rearrange("p (b t) -> p b t", b=2))
                last.then_inc(s_set, 1)
                dve.wait_ge(s_beta, bp * 2 + 2)
                dve.wait_ge(s_keep, bp * 2 + 2)
                n = PAST + NS
                V.tensor_tensor_scan(prod_s[:, n - 1:0:-1], keep_s[:, n - 1:0:-1], keep_s[:, n - 1:0:-1], 1.0,
                                     ALU.mult, ALU.bypass).then_inc(s_scan, 1)
                dve.wait_ge(s_scan, bp + 1)
                V.tensor_tensor(beta_s[:, 0:n - 1], beta_s[:, 0:n - 1], prod_s[:, 1:n], ALU.mult).then_inc(s_weighed, 1)
                dve.wait_ge(s_turned, bp + 1)
                V.tensor_copy(w_ts[:, 0:PAGES, :].rearrange("p a b -> p (a b)"), out[1][:, 2, 0:PAST])
                V.tensor_copy(w_ts[0:NS, PAGES, :], out[1][0:NS, 2, PAST:PAST + P]).then_inc(s_wt, 1)
                dve.wait_ge(s_full, bp + 3)
                for h in range(2):
                    rows = slice(DH * h, DH * h + DH)
                    o = mixed[rows, :, ds(bp * (2 * NT) + SEQ, 2 * NT)].rearrange("p c (b t) -> p b c t", b=2)
                    r = out[0][rows, 2, 0:P].rearrange("p (b c r) -> p b c r", b=2, c=KC)[:, :, :, h * NT:(h + 1) * NT]
                    last = V.tensor_copy(o, r)
                last.then_inc(s_out, 1)
            for n in range(2):
                V.memset(ext[n][:, 0:CW - 1], 0.0).then_inc(made, 1)
            dve.wait_ge(made, 7)
            split_mixed(H_WO)
            for f in range(KC):
                add_x(f, "wo", f, 0)
            norm("norm3", 3)
            ffn(1)
            norm("norm4", 4)


def kernel(**inputs):
    import numpy as np
    import ml_dtypes
    import concourse.bacc as bacc
    from concourse.bass_utils import run_bass_kernel_spmd

    a = {k: np.asarray(v) for k, v in inputs.items()}

    def by_features(v):
        v = v.reshape(v.shape[:-1] + (v.shape[-1] // P, P))
        return np.moveaxis(np.moveaxis(v, -1, 0), -1, 1)

    def tiles(w, order):
        k, n = w.shape
        t = w.reshape(k // P, P, n // P, P).transpose(2, 1, 0, 3).reshape(n // P, P, k)
        return t[order]

    tokens = np.concatenate([a["x_prompt"].reshape(SEQ, D), a["x_sample"].reshape(NS, D)])
    chunks = np.arange(KC)
    sc_in = tiles(a["w_sc_in"][0], np.stack([KC + chunks, 2 * KC + chunks, chunks], 1).ravel())
    qkv = tiles(a["w_qkv"][0], np.stack([2 * KC + chunks, chunks, KC + chunks], 1).ravel())

    def ffn(layer):
        hidden = np.arange(FC)
        up = tiles(a["w_ffn_up"][layer], np.stack([hidden, FC + hidden], 1).ravel())
        down = a["w_ffn_down"][layer].reshape(FC, P, D)
        rows = [up[0:4]]
        for g in range(1, PAIRS):
            rows += [up[4 * g:4 * g + 4], down[2 * g - 2:2 * g]]
        return rows + [down[FC - 2:]]

    weights = np.concatenate([sc_in, tiles(a["w_sc_out"][0], chunks), *ffn(0), qkv,
                              tiles(a["w_o"][0], chunks), *ffn(1)])
    gains = np.concatenate([np.stack([a["norm_mix"][0], a["norm_ffn"][0], a["norm_mix"][1], a["norm_ffn"][1],
                                      a["norm_final"]])])
    taps_sc = np.concatenate([a["w_sc_dw"][0], np.zeros((1, D), np.float32)])
    taps_ffn = np.concatenate([a["w_ffn_dw"], a["b_ffn_dw"][:, None, :]], 1)
    bf16 = ml_dtypes.bfloat16
    key, query = np.arange(P)[None, :], np.arange(P)[:, None]
    mask_diag = np.where(key < query, 0.0, MASKED).astype(bf16)
    row, new = np.arange(P)[:, None, None], np.arange(NS)[None, None, :]
    sample = 2 * np.arange(NB // 2)[None, :, None] + row // (P // 2)
    mask_new = np.where((new // NT == sample) & (new % NT < row % NT), 0.0, MASKED).astype(bf16)
    pool = a["cache_k"].shape[1]
    arrays = {
        "x_in": tokens.T.reshape(KC, P, T),
        "weights": weights,
        "taps_sc": by_features(taps_sc),
        "taps_ffn": by_features(taps_ffn).transpose(0, 2, 1, 3).reshape(P, 2 * FC, CW + 1),
        "state_sc": by_features(a["state_conv"][0]),
        "state_ffn": by_features(a["state_ffn"]).transpose(0, 2, 1, 3, 4).reshape(P, 2 * FC, NB, CW - 1),
        "gains": by_features(gains).transpose(0, 2, 1),
        "bias_heads": np.repeat(a["sb_bias"].reshape(1, H), P, 0),
        "bias_rows": np.tile(np.repeat(a["sb_bias"].reshape(H), NT), 2).reshape(P, 1),
        "cache_k": a["cache_k"][0].reshape(pool, PG, KC, P).transpose(0, 3, 2, 1),
        "cache_v": a["cache_v"][0].reshape(pool, PG, D),
        "pages": a["page_table"].reshape(1, NB * PAGES),
        "mask_diag": mask_diag,
        "mask_new": mask_new,
        "ident_in": np.eye(P, dtype=np.float32),
        "ident_b_in": np.eye(P, dtype=bf16),
    }
    arrays = {k: np.ascontiguousarray(v) for k, v in arrays.items()}
    outs = {"y_out": (KC, P, T), "k_out": (KC, P, T), "v_out": (KC, P, T),
            "conv_out": (P, KC, (1 + NB) * (CW - 1)), "ffn_out": (2, P, FC, (1 + NB) * (CW - 1))}
    nc = bacc.Bacc("TRN2", target_bir_lowering=False, num_devices=1)
    args = {k: nc.dram_tensor(k, v.shape, mybir.dt.from_np(v.dtype), kind="ExternalInput").ap()
            for k, v in arrays.items()}
    args |= {k: nc.dram_tensor(k, shape, mybir.dt.float32, kind="ExternalOutput").ap() for k, shape in outs.items()}
    build(nc, **args)
    got = run_bass_kernel_spmd(nc, [arrays], core_ids=[0]).results[0]

    def by_tokens(v):
        v = v.reshape(D, T).T
        return v[:SEQ], v[SEQ:]

    y_p, y_s = by_tokens(got["y_out"])
    k_p, k_s = by_tokens(got["k_out"])
    v_p, v_s = by_tokens(got["v_out"])

    def states(v):
        v = v.transpose(2, 1, 0).reshape((1 + NB) * (CW - 1), -1)
        return v[:CW - 1], v[CW - 1:].reshape(NB, CW - 1, -1)

    conv_p, conv_s = states(got["conv_out"])
    ffn_p, ffn_s = zip(*(states(v) for v in got["ffn_out"]), strict=True)
    return (y_p.reshape(1, SEQ, D), y_s.reshape(NB, NT, D),
            k_p.reshape(1, 1, SEQ, H, DH), v_p.reshape(1, 1, SEQ, H, DH),
            conv_p[None, None], np.stack(ffn_p)[:, None],
            k_s.reshape(1, NB, NT, H, DH), v_s.reshape(1, NB, NT, H, DH),
            conv_s[None], np.stack(ffn_s))
```

```python
import concourse.bass as bass
from concourse import mybir
from contextlib import ExitStack

P = 128
D = 1024
KC = D // P
SEQ = 1024
NB, NT = 8, 4
NS = NB * NT
T = SEQ + NS
TJ = 3
TW = T // TJ
F = 2816
FC = F // P
CW = 3
H, DH = 16, 64
PAGES, PG = 2, 128
PAST = PAGES * PG
EPS = 1e-6
MASKED = -1e30

N_SC_IN, N_SC_OUT, N_FFN, N_QKV, N_WO = 3 * KC, KC, 3 * FC, 3 * KC, KC
T_SC_IN = 0
T_SC_OUT = T_SC_IN + N_SC_IN
T_FFN0 = T_SC_OUT + N_SC_OUT
T_QKV = T_FFN0 + N_FFN
T_WO = T_QKV + N_QKV
T_FFN1 = T_WO + N_WO
N_TILES = T_FFN1 + N_FFN
RAW, SPLIT = 2, 3
UNROLL = RAW * SPLIT

PAIRS = FC // 2
FFN_TRIPS = (PAIRS - 1) // 2
FFN_OUT = 4 * PAIRS + KC * PAIRS
TRIP_FILLS = 4 + KC

FULL = {}
FREE = {}


def _count():
    full, free = [0, 0], [0, 0]

    def phase(name, full0, full1, free0=None, free1=None):
        FULL[name] = tuple(full)
        FREE[name] = tuple(free)
        full[0] += full0
        full[1] += full1
        free[0] += full0 if free0 is None else free0
        free[1] += full1 if free1 is None else free1

    phase("norm0", 1, 0)
    phase("sc_in", N_SC_IN // 2, N_SC_IN // 2)
    phase("sc_out", KC // 2, KC // 2)
    phase("norm1", 1, 0)
    phase("ffn0", FFN_OUT // 2, FFN_OUT // 2)
    phase("norm2", 1, 0)
    phase("qkv", 2 * KC, KC, 3 * KC, 2 * KC)
    phase("wo", KC // 2, KC // 2)
    phase("norm3", 1, 0)
    phase("ffn1", FFN_OUT // 2, FFN_OUT // 2)
    phase("norm4", 1, 0)


_count()
M_SC, M_FFN = 0, (KC, KC + FC)
H_SC_IN, H_SC_OUT, H_FFN0, H_QKV, H_WO, H_FFN1 = (KC * n for n in range(6))
QT = SEQ // P
TILE_ORDER = [i for n in range(QT // 2) for i in (QT - 1 - n, n)]
STEPS = [(i, h) for i in TILE_ORDER for h in range(2)]
UNITS = [(j, first, min(4, i + 1 - first)) for j, (i, h) in enumerate(STEPS) for first in range(0, i + 1, 4)]
BY_ACT = [STEPS[j][0] >= 4 and first == 0 for j, first, n in UNITS]
N_STEPS, N_UNITS = len(STEPS), len(UNITS)
Y_BY_DVE = 5


def copied(u):
    return BY_ACT[u], sum(a == BY_ACT[u] for a in BY_ACT[:u + 1])


def first_unit(j):
    return min(u for u in range(N_UNITS) if UNITS[u][0] == j)


def turned_by(j):
    return 1 + max(u for u in range(N_UNITS) if UNITS[u][0] == j)




def build(nc, x_in, weights, taps_sc, taps_ffn, state_sc, state_ffn, gains, bias_heads, bias_rows,
          cache_k, cache_v, pages, mask_diag, mask_new, ident_in, ident_b_in,
          y_out, k_out, v_out, conv_out, ffn_out):
    f32, f32r, bf16, i32 = mybir.dt.float32, mybir.dt.float32r, mybir.dt.bfloat16, mybir.dt.int32
    ACT, ALU = mybir.ActivationFunctionType, mybir.AluOpType
    ds = bass.ds
    ctx = ExitStack()
    with ctx:
        base = -(-nc.sbuf_base // 64) * 64
        arena = nc.sbuf_usable_end - base
        arena -= arena % 64
        ctx.enter_context(nc.sbuf_tensor("arena", [P, arena // 4], f32))
        top = [base]

        def at(offset, name, shape, dt):
            return nc.alloc_sbuf_tensor_at(name, shape, dt, offset=offset)

        def size(shape, dt):
            n = 1
            for d in shape[1:]:
                n *= d
            return -(-n * (2 if dt == bf16 else 4) // 32) * 32

        def sb(name, shape, dt=f32):
            t = at(top[0], name, shape, dt)
            top[0] += size(shape, dt)
            assert top[0] <= base + arena, name
            return t

        x = sb("x", [P, KC, T])
        h_at = top[0]
        h_hi = sb("h_hi", [P, KC, T], f32r)
        h_lo = sb("h_lo", [P, KC, T], f32r)
        h_end = top[0]
        raw = [sb(f"raw{n}", [P, D]) for n in range(RAW)]
        w_hi = [sb(f"w_hi{n}", [P, D], f32r) for n in range(SPLIT)]
        w_lo = [sb(f"w_lo{n}", [P, D], f32r) for n in range(SPLIT)]
        mean = sb("mean", [P, P])
        ident = sb("ident", [P, P])
        ident_b = sb("ident_b", [P, P], bf16)
        diag_b = sb("diag_b", [P, P], bf16)
        new_b = sb("new_b", [P, NB // 2, NS], bf16)
        gain = sb("gain", [P, 5, KC])
        tap_sc = sb("tap_sc", [P, KC, CW + 1])
        tap_ffn = sb("tap_ffn", [P, 2 * FC, CW + 1])
        st_sc = sb("st_sc", [P, KC, NB, CW - 1])
        st_ffn = sb("st_ffn", [P, 2 * FC, NB, CW - 1])
        new_sc = sb("new_sc", [P, KC, (1 + NB) * (CW - 1)])
        new_ffn = sb("new_ffn", [P, FC, (1 + NB) * (CW - 1)])
        bias_h = sb("bias_h", [P, 2, H])
        bias_r = sb("bias_r", [P, 2])
        eps = sb("eps", [P, 1])
        bias_now = [sb(f"bias_now{n}", [P, 1]) for n in range(2)]
        bias_pair = sb("bias_pair", [P, 2, 2])
        page_row = sb("page_row", [1, NB * PAGES], i32)
        rstd = sb("rstd", [P, T])
        overlay = top[0]
        mixed = sb("mixed", [P, KC, T])
        after_mixed = top[0]
        ext = [sb(f"ext{n}", [P, T + CW - 1]) for n in range(2)]
        smp = [sb(f"smp{n}", [P, NB, CW - 1 + NT]) for n in range(2)]
        y = [sb(f"y{n}", [P, T]) for n in range(2)]
        square = [sb(f"square{n}", [P, T]) for n in range(2)]
        total = sb("total", [P, T])
        c_gate = [sb(f"c_gate{n}", [P, T]) for n in range(2)]
        rstd2 = total
        top[0] = overlay
        a_hi = sb("a_hi", [P, 2, 2, T], f32r)
        a_lo = sb("a_lo", [P, 2, 2, T], f32r)
        assert top[0] == after_mixed
        q_t = sb("q_t", [P, T])
        k_t = sb("k_t", [P, T])
        v_t = sb("v_t", [P, T])
        v_rows = sb("v_rows", [P, QT, P])
        q_s = sb("q_s", [P, KC, NS])
        k_s = sb("k_s", [P, KC, NS])
        v_s = sb("v_s", [P, KC, NS])
        after_s = top[0]
        beta = [sb(f"beta{n}", [P, SEQ]) for n in range(2)]
        keep = [sb(f"keep{n}", [P, SEQ]) for n in range(2)]
        prod = sb("prod", [P, SEQ])
        w_t = [sb(f"w_t{n}", [P, 4, P]) for n in range(2)]
        top[0] = h_at
        page_k = [sb(f"page_k{n}", [P, KC, PAGES, PG]) for n in range(4)]
        page_v = [sb(f"page_v{n}", [P, PAGES, D]) for n in range(4)]
        assert top[0] <= h_end
        top[0] = after_mixed
        q_rows = [sb(f"q_rows{n}", [P, KC * (P + 2 * NT)]) for n in range(2)]
        assert top[0] <= after_s - 3 * size(q_s.shape, f32)
        top[0] = after_s
        v_new = sb("v_new", [NS, D])
        o_rows = sb("o_rows", [P, D])
        beta_s = [sb(f"beta_s{n}", [P, PAST + NS]) for n in range(2)]
        keep_s = [sb(f"keep_s{n}", [P, PAST + NS]) for n in range(2)]
        prod_s = sb("prod_s", [P, PAST + NS])
        w_ts = sb("w_ts", [P, PAGES + 1, P])
        y_rows = at(h_at, "y_rows", [P, KC, T], f32)

        bank = [ctx.enter_context(nc.psum_tensor(f"bank{n}", [P, 3 if n < 2 else 2, 512], f32)) for n in range(3)]
        out = [bank[0], bank[1]]
        spare = bank[2]

        def result(s):
            return out[s][:, :, 0:TW]

        score = [out[1][:, 0:2, :].rearrange("p a b -> p (a b)"), spare[:, :, :].rearrange("p a b -> p (a b)")]
        turned = [out[1][:, 2, :], out[0][:, 2, :]]
        attended = out[0][:, 0:2, :].rearrange("p a b -> p (a b)")

        def sem(name):
            return ctx.enter_context(nc.semaphore(name))

        raw_loaded = [sem(f"raw_loaded{n}") for n in range(RAW)]
        w_high = sem("w_high")
        w_split = sem("w_split")
        w_used = sem("w_used")
        full = [sem("full0"), sem("full1")]
        taken = [sem("taken0"), sem("taken1")]
        x_loaded = [sem(f"x_loaded{f}") for f in range(KC)]
        gain_loaded = sem("gain_loaded")
        squared_rstd = sem("squared_rstd")
        c_scaled = sem("c_scaled")
        y_scaled = sem("y_scaled")
        s_o_rows = sem("s_o_rows")
        s_o_turned = sem("s_o_turned")
        y_gained = sem("y_gained")
        y_by_pool = sem("y_by_pool")
        consts = sem("consts")
        state_loaded = sem("state_loaded")
        made = sem("made")
        kv_free = sem("kv_free")
        negated = sem("negated")
        rstd_made = sem("rstd_made")
        bias_set = sem("bias_set")
        pair_bias_set = sem("pair_bias_set")
        split_begun = sem("split_begun")
        new_copied = sem("new_copied")
        squared = sem("squared")
        summed = sem("summed")
        h_high = sem("h_high")
        h_ready = sem("h_ready")
        smp_full = sem("smp_full")
        tapped = sem("tapped")
        convolved = sem("convolved")
        silued = sem("silued")
        a_high = sem("a_high")
        a_ready = sem("a_ready")
        kv_stored = sem("kv_stored")
        v_turned = sem("v_turned")
        v_ready = sem("v_ready")
        scored = sem("scored")
        beta_done = sem("beta_done")
        keep_done = sem("keep_done")
        scanned = sem("scanned")
        weighed = sem("weighed")
        turn_done = sem("turn_done")
        w_t_by_act = sem("w_t_by_act")
        w_t_by_dve = sem("w_t_by_dve")
        pv_done = sem("pv_done")
        page_in = [sem(f"page_in{n}") for n in range(4)]
        page_ids = sem("page_ids")
        s_set = sem("s_set")
        s_scored = sem("s_scored")
        s_beta = sem("s_beta")
        s_keep = sem("s_keep")
        s_scan = sem("s_scan")
        s_weighed = sem("s_weighed")
        s_turned = sem("s_turned")
        s_wt = sem("s_wt")
        s_full = sem("s_full")
        s_vturned = sem("s_vturned")
        s_vnew = sem("s_vnew")
        s_out = sem("s_out")
        y_made = sem("y_made")
        stored = sem("stored")

        block = ctx.enter_context(nc.Block())

        @block.sync
        def _(sp):
            def load_tile(n, slot):
                sp.wait_ge(w_split, n + 1)
                sp.dma_start(raw[slot][:, :], weights[ds(n, 1), :, :].rearrange("o p n -> p (o n)")).then_inc(raw_loaded[slot], 16)

            sp.sem_inc(w_split, RAW)
            sp.sem_inc(s_full, 2)
            sp.dma_start(page_row[:, :], pages).then_inc(page_ids, 16)
            sp.wait_ge(page_ids, 16)
            early = T_WO + SPLIT + 1
            assert early % UNROLL == 0
            with sp.Fori(0, early // UNROLL) as i:
                for u in range(UNROLL):
                    load_tile(i * UNROLL + u, u % RAW)
            sp.wait_ge(taken[0], FREE["qkv"][0] + 3 * (KC - 1) + 2 + 1)
            with sp.Fori(0, 2) as i:
                for n in range(4):
                    sp.wait_ge(s_full, i * 2 + (n // 2 + 1))
                    for g in range(PAGES):
                        page = sp.value_load(page_row[0:1, ds(i * 8 + n * PAGES + g, 1)],
                                             min_val=0, max_val=cache_k.shape[0] - 1)
                        sp.dma_start(page_k[n][:, :, g, :], cache_k[ds(page, 1), :, :, :].rearrange("o p c t -> p (o c) t")).then_inc(page_in[n], 16)
                        sp.dma_start(page_v[n][:, g, :], cache_v[ds(page, 1), :, :].rearrange("o p n -> p (o n)")).then_inc(page_in[n], 16)
            rest = N_TILES - early
            with sp.Fori(0, rest // UNROLL) as i:
                for u in range(UNROLL):
                    load_tile(i * UNROLL + (early + u), u % RAW)
            for n in range(rest - rest % UNROLL, rest):
                load_tile(early + n, n % RAW)

        @block.gpsimd
        def _(pool):
            def split_tile(n, slot, ring, nth):
                pool.wait_ge(raw_loaded[slot], nth * 16)
                pool.wait_ge(w_used, n + 1)
                pool.sem_inc(split_begun, 1)
                nc.gpsimd.tensor_copy(w_hi[ring][:, :], raw[slot][:, :]).then_inc(w_high, 1)
                pool.wait_ge(w_high, n + 1)
                nc.gpsimd.tensor_tensor(w_lo[ring][:, :], raw[slot][:, :], w_hi[ring][:, :].bitcast(f32),
                                        ALU.subtract).then_inc(w_split, 1)

            pool.sem_inc(w_used, SPLIT - 1)
            with pool.Fori(0, N_TILES // UNROLL) as i:
                for u in range(UNROLL):
                    split_tile(i * UNROLL + u, u % RAW, u % SPLIT, i * (UNROLL // RAW) + (u // RAW + 1))
            for n in range(N_TILES - N_TILES % UNROLL, N_TILES):
                split_tile(n, n % RAW, n % SPLIT, n // RAW + 1)
            pool.wait_ge(rstd_made, 5)
            for f in range(Y_BY_DVE, KC):
                pool.wait_ge(y_gained, f + 1)
                nc.gpsimd.tensor_tensor(y_rows[:, f, :], y_rows[:, f, :], rstd[:, :], ALU.mult).then_inc(y_by_pool, 1)

        @block.tensor
        def _(pe):
            def three(o, w, c0, hi, lo, first, last, counts=False):
                mm = nc.tensor.matmul(o, w_hi[w][:, c0:c0 + P], hi, start=first, stop=False)
                if counts:
                    mm.then_inc(w_used, 1)
                nc.tensor.matmul(o, w_hi[w][:, c0:c0 + P], lo, start=False, stop=False)
                return nc.tensor.matmul(o, w_lo[w][:, c0:c0 + P], hi, start=False, stop=last)

            def norm_sum(name, nth):
                pe.wait_ge(summed, KC * (nth + 1))
                pe.wait_ge(taken[0], FREE[name][0] + 1)
                for j in range(TJ):
                    mm = nc.tensor.matmul(out[0][:, j, 0:TW], mean[:, :], total[:, j * TW:(j + 1) * TW],
                                          start=True, stop=True)
                mm.then_inc(full[0], 1)

            def linear(tile, ring, s, fill, h_base=None, midway=None):
                pe.wait_ge(w_split, tile + (RAW + 1))
                pe.wait_ge(taken[s], fill + 1)
                for k in range(KC):
                    if h_base is not None:
                        pe.wait_ge(h_ready, h_base + k + 1)
                    for j in range(TJ):
                        mm = three(out[s][:, j, 0:TW], ring, k * P, h_hi[:, k, j * TW:(j + 1) * TW],
                                   h_lo[:, k, j * TW:(j + 1) * TW], k == 0, k == KC - 1,
                                   k == j == 0)
                    if k == KC // 2 and midway is not None:
                        midway()
                mm.then_inc(full[s], 1)

            def tiles_of(name, tile0, h_base):
                for k in range(KC):
                    s = (k + 1) % 2
                    linear(tile0 + k, (tile0 + k) % SPLIT, s, FREE[name][s] + k // 2,
                           h_base if k == 0 else None)

            def up(tile, ring0, k0, name, trip, h_base=None, norm=None):
                for n in range(4):
                    s = (k0 + n + 1) % 2
                    linear(tile + n, (ring0 + n) % SPLIT, s, trip * TRIP_FILLS + (FREE[name][s] + (k0 + n) // 2),
                           h_base if n == 0 else None)
                    if n == 0 and norm is not None:
                        norm_sum(f"norm{norm}", norm)

            def down(tile, ring0, k0, name, trip, slot, group):
                pe.wait_ge(w_split, tile + (RAW + 2))
                pe.wait_ge(a_ready, group * 2 + 4)
                for f in range(KC):
                    s = (k0 + f + 1) % 2
                    pe.wait_ge(taken[s], trip * TRIP_FILLS + (FREE[name][s] + (k0 + f) // 2 + 1))
                    for kk in range(2):
                        for j in range(TJ):
                            mm = three(out[s][:, j, 0:TW], (ring0 + kk) % SPLIT, f * P,
                                       a_hi[:, slot, kk, j * TW:(j + 1) * TW],
                                       a_lo[:, slot, kk, j * TW:(j + 1) * TW], kk == 0, kk == 1,
                                       j == 0 and (f, kk) in ((0, 0), (KC - 1, 1)))
                    mm.then_inc(full[s], 1)

            def ffn(layer):
                name = f"ffn{layer}"
                t0 = (T_FFN0, T_FFN1)[layer]
                g0 = layer * PAIRS
                up(t0, t0, 0, name, 0, (H_FFN0, H_FFN1)[layer], (1, 3)[layer])
                with pe.Fori(0, FFN_TRIPS) as i:
                    for n in range(2):
                        r0 = t0 + 4 + 6 * n
                        k0 = 4 + (4 + KC) * n
                        up(i * 12 + r0, r0, k0, name, i)
                        down(i * 12 + (r0 + 4), r0 + 4, k0 + 4, name, i, n, i * 2 + (g0 + n))
                last = 4 + 6 * (PAIRS - 1)
                down(t0 + last, t0 + last, 4 + (4 + KC) * (PAIRS - 1), name, 0, 0, g0 + PAIRS - 1)

            pe.wait_ge(made, 1)

            def sc_in(trip, first):
                for n in range(6):
                    s = (n + 1) % 2
                    linear(trip * 6 + n, n % SPLIT, s, trip * 3 + (FREE["sc_in"][s] + n // 2),
                           H_SC_IN if first and n == 0 else None)
                    if first and n == 0:
                        norm_sum("norm0", 0)

            sc_in(0, True)
            with pe.Fori(1, KC // 2) as i:
                sc_in(i, False)
            tiles_of("sc_out", T_SC_OUT, H_SC_OUT)
            ffn(0)

            def scores(pair, j):
                i, h = STEPS[j]
                rows = slice(DH * h, DH * h + DH)
                pe.wait_ge(keep_done, pair * N_STEPS + (j + 1))
                width = P * (i + 1)
                for n0 in range(0, width, 512):
                    n1 = min(n0 + 512, width)
                    nc.tensor.matmul(score[j % 2][:, n0:n1], q_t[rows, i * P:(i + 1) * P], k_t[rows, n0:n1],
                                     start=True, stop=n1 < width)
                nc.tensor.matmul(score[j % 2][:, width - P:width], ident_b[:, :], diag_b[:, :],
                                 start=False, stop=True).then_inc(scored, 1)

            def unit_copied(pair, u):
                by_act, n = copied(u)
                if by_act:
                    pe.wait_ge(w_t_by_act, pair * sum(BY_ACT) + n)
                else:
                    pe.wait_ge(w_t_by_dve, pair * (N_UNITS - sum(BY_ACT)) + n)

            def turn(pair, u):
                j, first, n = UNITS[u]
                pe.wait_ge(weighed, pair * N_STEPS + (j + 2))
                if u >= 2:
                    unit_copied(pair, u - 2)
                for b in range(n):
                    mm = nc.tensor.transpose(turned[u % 2][:, b * P:(b + 1) * P],
                                             beta[j % 2][:, (first + b) * P:(first + b + 1) * P], ident[:, :])
                mm.then_inc(turn_done, 1)

            def values(pair, u):
                j, first, n = UNITS[u]
                i, h = STEPS[j]
                unit_copied(pair, u)
                for b in range(n):
                    mm = nc.tensor.matmul(attended[DH * h:DH * h + DH, i * P:(i + 1) * P],
                                          v_rows[:, first + b, DH * h:DH * h + DH], w_t[u % 2][:, b, :],
                                          start=first + b == 0, stop=first + b == i)
                mm.then_inc(pv_done, 1)

            norm_sum("norm2", 2)
            with pe.Fori(0, KC) as c:
                tile = c * 3 + T_QKV
                f0 = c * 3 + FREE["qkv"][0]
                f1 = c * 2 + FREE["qkv"][1]

                def first_scores():
                    pe.wait_ge(taken[0], f0 + 2)
                    pe.wait_ge(taken[1], f1 + 2)
                    scores(c, 0)
                    scores(c, 1)

                linear(tile, T_QKV % SPLIT, 0, f0, H_QKV)
                linear(tile + 1, (T_QKV + 1) % SPLIT, 1, f1)
                linear(tile + 2, (T_QKV + 2) % SPLIT, 0, f0 + 1, None, first_scores)
                pe.wait_ge(taken[0], f0 + 3)
                for b in range(QT):
                    mm = nc.tensor.transpose(attended[:, b * P:(b + 1) * P], v_t[:, b * P:(b + 1) * P], ident[:, :])
                mm.then_inc(v_turned, 1)
                turn(c, 0)
                scores(c, 2)
                for u in range(N_UNITS):
                    if u + 1 < N_UNITS:
                        turn(c, u + 1)
                        j, first, _ = UNITS[u + 1]
                        if first == 0 and j + 2 < N_STEPS:
                            scores(c, j + 2)
                    if u == 0:
                        pe.wait_ge(v_ready, c + 1)
                    values(c, u)

            pe.wait_ge(taken[0], FREE["wo"][0] + 1)
            pe.wait_ge(taken[1], FREE["wo"][1] + 1)
            for c in range(KC):
                mm = nc.tensor.transpose(score[1][0:NS, c * P:(c + 1) * P], v_s[:, c, :], ident[:, :])
            mm.then_inc(s_vturned, 1)

            def sample_scores(bp):
                pe.wait_ge(s_set, bp + 1)
                bank_s = out[1][:, bp % 2, :]
                for b in range(2):
                    slot, rows = 2 * (bp % 2) + b, slice(64 * b, 64 * b + 64)
                    pe.wait_ge(page_in[slot], (bp // 2 + 1) * 64)
                    for new in range(2):
                        for c in range(KC):
                            q = q_rows[bp % 2][:, c * P + 64 * b:c * P + 64 * b + 64]
                            keys = k_s[:, c, :] if new else page_k[slot][:, c, :, :].rearrange("p g t -> p (g t)")
                            o = bank_s[rows, PAST:PAST + NS] if new else bank_s[rows, 0:PAST]
                            nc.tensor.matmul(o, q, keys, start=c == 0, stop=c == KC - 1, skip_group_check=True)
                nc.tensor.matmul(bank_s[:, PAST:PAST + NS], ident_b[:, :], new_b[:, bp, :], start=False,
                                 stop=True, skip_group_check=True).then_inc(s_scored, 1)

            def sample_turn(bp):
                pe.wait_ge(s_weighed, bp + 1)
                w = beta_s[bp % 2]
                for g in range(PAGES):
                    nc.tensor.transpose(out[1][:, 2, g * P:(g + 1) * P], w[:, g * P:(g + 1) * P], ident[:, :])
                nc.tensor.transpose(out[1][0:NS, 2, PAST:PAST + P], w[:, PAST:PAST + NS],
                                    ident[:, :]).then_inc(s_turned, 1)

            def sample_values(bp):
                pe.wait_ge(s_wt, bp + 1)
                if bp:
                    pe.wait_ge(s_o_rows, bp)
                for b in range(2):
                    slot, rows = 2 * (bp % 2) + b, slice(64 * b, 64 * b + 64)
                    for half in range(2):
                        o, cols = out[0][rows, half, :], slice(512 * half, 512 * half + 512)
                        for g in range(PAGES):
                            nc.tensor.matmul(o, w_ts[:, g, rows], page_v[slot][:, g, cols], start=g == 0, stop=False)
                        mm = nc.tensor.matmul(o, w_ts[0:NS, PAGES, rows], v_new[:, cols], start=False, stop=True)
                mm.then_inc(s_full, 1)

            def sample_out(bp):
                pe.wait_ge(s_o_rows, bp + 1)
                pe.wait_ge(s_out, bp + 1)
                for c in range(KC):
                    mm = nc.tensor.transpose(score[1][:, c * P:(c + 1) * P], o_rows[:, c * P:(c + 1) * P], ident[:, :])
                mm.then_inc(s_o_turned, 1)

            sample_scores(0)
            pe.wait_ge(s_vnew, 1)
            for bp in range(NB // 2):
                if bp + 1 < NB // 2:
                    sample_scores(bp + 1)
                if bp:
                    sample_out(bp - 1)
                sample_turn(bp)
                sample_values(bp)
            sample_out(NB // 2 - 1)
            pe.wait_ge(s_out, NB // 2 + 1)
            tiles_of("wo", T_WO, H_WO)
            ffn(1)
            norm_sum("norm4", 4)

        @block.scalar
        def _(act):
            def act_op(o, i, func=ACT.Copy, **kw):
                return nc.scalar.activation(o, i, func, **kw)

            act.dma_start(gain[:, :, :], gains).then_inc(gain_loaded, 16)
            for f in range(KC):
                act.dma_start(x[:, f, :], x_in[f, :, :]).then_inc(x_loaded[f], 16)
            act.dma_start(tap_sc[:, :, :], taps_sc).then_inc(consts, 16)
            act.dma_start(tap_ffn[:, :, :], taps_ffn).then_inc(consts, 16)
            act.dma_start(ident[:, :], ident_in).then_inc(consts, 16)
            act.dma_start(ident_b[:, :], ident_b_in).then_inc(consts, 16)
            act.dma_start(diag_b[:, :], mask_diag).then_inc(consts, 16)
            act.dma_start(new_b[:, :, :], mask_new).then_inc(consts, 16)
            act.dma_start(bias_h[:, 0, :], bias_heads).then_inc(consts, 16)
            act.dma_start(bias_r[:, 0:1], bias_rows).then_inc(consts, 16)
            act.dma_start(st_sc[:, :, :, :], state_sc).then_inc(state_loaded, 16)
            act.dma_start(st_ffn[:, :, :, :], state_ffn).then_inc(state_loaded, 16)
            act.sem_inc(convolved, 2)

            def norm(nth, layer_before, k_before, h_first):
                def ready(f):
                    if nth == 0:
                        act.wait_ge(x_loaded[f], 16)
                    else:
                        k = k_before + f
                        s = (k + 1) % 2
                        act.wait_ge(taken[s], FREE[layer_before][s] + k // 2 + 2)

                def high(f):
                    act_op(h_hi[:, f, :], x[:, f, :], scale=gain[:, nth, f:f + 1]).then_inc(h_high, 1)

                def square_of(f):
                    if f >= 2:
                        act.wait_ge(summed, KC * nth + f - 1)
                    act_op(square[f % 2][:, :], x[:, f, :], ACT.Square).then_inc(squared, 1)

                for f in range(KC):
                    ready(f)
                    if nth == 4 or (not h_first and f < KC - 1):
                        square_of(f)
                    elif h_first:
                        high(f)
                if h_first:
                    for f in range(KC):
                        square_of(f)
                elif nth == 2:
                    square_of(KC - 1)
                    for f in range(KC):
                        high(f)
                elif nth < 4:
                    for f in range(KC):
                        high(f)
                    square_of(KC - 1)
                if nth == 4:
                    for f in range(KC):
                        act_op(y_rows[:, f, :], x[:, f, :], scale=gain[:, nth, f:f + 1]).then_inc(y_gained, 1)
                act.wait_ge(full[0], FULL[f"norm{nth}"][0] + 1)
                act_op(total[:, :].rearrange("p (a b) -> p a b", a=TJ), result(0), ACT.Sqrt,
                       bias=eps[:, 0:1]).then_inc(taken[0], 1)

            def split_mixed():
                for f in range(KC):
                    act_op(h_hi[:, f, :], mixed[:, f, :]).then_inc(h_high, 1)

            def samples(m, par, states, kept):
                tokens = ext[par][:, CW - 1 + SEQ:CW - 1 + T].rearrange("p (b t) -> p b t", t=NT)
                act_op(smp[par][:, :, CW - 1:], tokens).then_inc(smp_full, 1)
                act_op(smp[par][:, :, 0:CW - 1], states).then_inc(smp_full, 1)
                act_op(kept[:, 0:CW - 1], ext[par][:, SEQ:SEQ + CW - 1]).then_inc(smp_full, 1)
                act_op(kept[:, CW - 1:].rearrange("p (b t) -> p b t", t=CW - 1),
                       tokens[:, :, NT - CW + 1:]).then_inc(smp_full, 1)

            def ffn_chunk(m, par, chunk, layer, k, trip, slot, group):
                name = f"ffn{layer}"
                s = (k + 1) % 2
                act.wait_ge(taken[s], trip * TRIP_FILLS + (FREE[name][s] + k // 2 + 2))
                samples(m, par, st_ffn[:, ds(chunk + layer * FC, 1), :, :].rearrange("p o b t -> p (o b) t"),
                        new_ffn[:, ds(chunk, 1), :].rearrange("p o t -> p (o t)"))
                act_op(bias_now[par][:, :], tap_ffn[:, ds(chunk + layer * FC, 1), CW:CW + 1].rearrange("p o t -> p (o t)")
                       ).then_inc(bias_set, 1)
                act.wait_ge(bias_set, m - (KC - 1))
                act.wait_ge(convolved, m + 3)
                act_op(y[par][:, :], y[par][:, :], ACT.Silu, bias=bias_now[par][:, :]).then_inc(silued, 1)
                s = (k + 2) % 2
                act.wait_ge(taken[s], trip * TRIP_FILLS + (FREE[name][s] + (k + 1) // 2 + 2))
                if par == 0 and group is not None:
                    act.wait_ge(taken[0], group)
                act_op(a_hi[:, slot, par, :], y[par][:, :]).then_inc(a_high, 1)

            def ffn(layer):
                name = f"ffn{layer}"
                m0 = M_FFN[layer]
                for p in range(2):
                    ffn_chunk(m0 + p, p, p, layer, 2 * p, 0, 0, None)
                with act.Fori(0, FFN_TRIPS) as i:
                    for n in range(2):
                        k0 = (4 + KC) * n + 4
                        for p in range(2):
                            ffn_chunk(i * 4 + (m0 + 2 + 2 * n + p), p, i * 4 + (2 + 2 * n + p), layer,
                                      k0 + 2 * p, i, (n + 1) % 2, i * TRIP_FILLS + (FREE[name][0] + (k0 - 1) // 2 + 2))
                act.wait_ge(smp_full, 4 * (m0 + FC))
                act.dma_start(ffn_out[layer], new_ffn[:, :, :]).then_inc(stored, 16)

            act.wait_ge(gain_loaded, 16)
            act.wait_ge(made, 2)
            norm(0, None, 0, True)
            act.wait_ge(state_loaded, 32)
            act.wait_ge(consts, 16 * 8)
            act_op(bias_h[:, 1, :], bias_h[:, 0, :], scale=-1.0).then_inc(negated, 1)
            act_op(bias_r[:, 1:2], bias_r[:, 0:1], scale=-1.0).then_inc(negated, 1)
            with act.Fori(0, KC // 2) as i:
                for n in range(2):
                    k = 3 * n
                    s = (k + 1) % 2
                    m = i * 2 + n
                    act.wait_ge(convolved, m + 1)
                    act.wait_ge(full[s], i * 3 + (FULL["sc_in"][s] + k // 2 + 1))
                    act_op(c_gate[n][:, :].rearrange("p (a b) -> p a b", a=TJ), result(s)).then_inc(taken[s], 1)
                    s = (k + 2) % 2
                    act.wait_ge(taken[s], i * 3 + (FREE["sc_in"][s] + (k + 1) // 2 + 2))
                    samples(m, n, st_sc[:, ds(m, 1), :, :].rearrange("p o b t -> p (o b) t"),
                            new_sc[:, ds(m, 1), :].rearrange("p o t -> p (o t)"))
            act.wait_ge(smp_full, 4 * KC)
            act.dma_start(conv_out, new_sc[:, :, :]).then_inc(stored, 16)
            act.wait_ge(taken[0], FREE["sc_out"][0] + 1)
            split_mixed()
            norm(1, "sc_out", 0, False)
            act.preload_act_table(ACT.Silu)
            ffn(0)
            norm(2, "ffn0", FFN_OUT - KC, False)

            act.wait_ge(negated, 2)
            act.preload_act_table(ACT.Sigmoid)
            with act.Fori(0, KC) as c:
                def new_tokens(dst, src):
                    act_op(dst[:, ds(c, 1), :].rearrange("p o t -> p (o t)"), src[:, SEQ:T]).then_inc(new_copied, 1)

                def sigmoids(j):
                    i, h = STEPS[j]
                    width = P * (i + 1)
                    act.wait_ge(scored, c * N_STEPS + (j + 1))
                    if j >= 2:
                        act.wait_ge(turn_done, c * N_UNITS + turned_by(j - 2))
                    act_op(beta[j % 2][:, 0:width], score[j % 2][:, 0:width], ACT.Sigmoid,
                           bias=bias_pair[:, 0, h:h + 1]).then_inc(beta_done, 1)
                    act.wait_ge(scanned, c * N_STEPS + (j + 1))
                    act_op(keep[j % 2][:, 0:width], score[j % 2][:, 0:width], ACT.Sigmoid, scale=-1.0,
                           bias=bias_pair[:, 1, h:h + 1]).then_inc(keep_done, 1)

                def copy_turned(u):
                    act.wait_ge(turn_done, c * N_UNITS + (u + 1))
                    if u >= 2:
                        act.wait_ge(pv_done, c * N_UNITS + (u - 1))
                    n = UNITS[u][2]
                    act_op(w_t[u % 2][:, 0:n, :].rearrange("p a b -> p (a b)"),
                           turned[u % 2][:, 0:n * P]).then_inc(w_t_by_act, 1)

                act.wait_ge(taken[0], c * 3 + (FREE["qkv"][0] + 2))
                act_op(bias_pair[:, :, :], bias_h[:, :, ds(c * 2, 2)]).then_inc(pair_bias_set, 1)
                new_tokens(q_s, q_t)
                act.wait_ge(taken[1], c * 2 + (FREE["qkv"][1] + 2))
                act.dma_start(k_out[ds(c, 1), :, :].rearrange("o p t -> p (o t)"), k_t[:, :]).then_inc(kv_stored, 16)
                new_tokens(k_s, k_t)
                act.wait_ge(new_copied, c * 3 + 2)
                act.wait_ge(pair_bias_set, c + 1)
                sigmoids(0)
                sigmoids(1)
                act.wait_ge(taken[0], c * 3 + (FREE["qkv"][0] + 3))
                act.dma_start(v_out[ds(c, 1), :, :].rearrange("o p t -> p (o t)"), v_t[:, :]).then_inc(kv_stored, 16)
                new_tokens(v_s, v_t)
                act.wait_ge(v_turned, c + 1)
                act_op(v_rows[:, :, :].rearrange("p a b -> p (a b)"), attended).then_inc(v_ready, 1)
                for j in range(N_STEPS):
                    if BY_ACT[first_unit(j)]:
                        copy_turned(first_unit(j))
                    if j + 2 < N_STEPS:
                        sigmoids(j + 2)
                act.wait_ge(kv_stored, c * 32 + 32)
                act.wait_ge(new_copied, c * 3 + 3)
                act.sem_inc(kv_free, 1)
            def sample_sigmoids(bp):
                act.wait_ge(s_scored, bp + 1)
                z = out[1][:, bp % 2, 0:PAST + NS]
                act_op(beta_s[bp % 2][:, :], z, ACT.Sigmoid, bias=bias_r[:, 0:1]).then_inc(s_beta, 1)
                act_op(keep_s[bp % 2][:, :], z, ACT.Sigmoid, scale=-1.0, bias=bias_r[:, 1:2]).then_inc(s_keep, 1)

            def sample_rows(bp):
                act.wait_ge(s_full, bp + 3)
                act_op(o_rows[:, :], attended).then_inc(s_o_rows, 1)

            sample_sigmoids(0)
            for bp in range(NB // 2):
                if bp + 1 < NB // 2:
                    sample_sigmoids(bp + 1)
                sample_rows(bp)
            act.wait_ge(s_out, NB // 2 + 1)
            split_mixed()
            norm(3, "wo", 0, False)
            act.preload_act_table(ACT.Silu)
            ffn(1)
            norm(4, "ffn1", FFN_OUT - KC, False)
            for n in range(KC):
                f = {0: 0, 1: 1, 2: Y_BY_DVE, 3: 2, 4: 3, 5: Y_BY_DVE + 1, 6: 4, 7: Y_BY_DVE + 2}[n]
                if f < Y_BY_DVE:
                    act.wait_ge(y_made, f + 1)
                else:
                    act.wait_ge(y_by_pool, f - Y_BY_DVE + 1)
                act.dma_start(y_out[f, :, :], y_rows[:, f, :]).then_inc(stored, 16)
            act.wait_ge(stored, 16 * (3 + KC))
            act.wait_ge(kv_stored, 32 * KC)

        @block.vector
        def _(dve):
            V = nc.vector

            for s in range(2):
                dve.sem_inc(taken[s], 1)
            dve.sem_inc(scanned, 2)
            dve.sem_inc(keep_done, 2)
            dve.sem_inc(kv_free, 1)
            dve.sem_inc(s_out, 1)
            dve.sem_inc(a_ready, 2)
            dve.sem_inc(weighed, 1)
            V.memset(mean[:, :], 1.0 / D).then_inc(made, 1)
            V.memset(eps[:, :], EPS).then_inc(made, 1)
            for n in range(2):
                V.memset(ext[n][:, 0:CW - 1], 0.0).then_inc(made, 1)

            def wide(t):
                return t.rearrange("p (a b) -> p a b", a=TJ)

            def norm(nth, add, h_first):
                def low(f):
                    dve.wait_ge(h_high, H_BASE[nth] + f + 1)
                    V.scalar_tensor_tensor(h_lo[:, f, :], x[:, f, :], gain[:, nth, f:f + 1],
                                           h_hi[:, f, :].bitcast(f32), ALU.mult, ALU.subtract).then_inc(h_ready, 1)

                def sum_up(f):
                    n = KC * nth + f
                    dve.wait_ge(squared, n + 1)
                    if f == 0:
                        V.tensor_copy(total[:, :], square[0][:, :]).then_inc(summed, 1)
                    else:
                        dve.wait_ge(summed, n)
                        V.tensor_tensor(total[:, :], total[:, :], square[f % 2][:, :], ALU.add).then_inc(summed, 1)

                for f in range(KC):
                    add(f)
                    if h_first and f:
                        low(f - 1)
                    elif not h_first and f < KC - 1:
                        sum_up(f)
                if h_first:
                    low(KC - 1)
                    for f in range(KC):
                        sum_up(f)
                elif nth == 2:
                    sum_up(KC - 1)
                    for f in range(KC):
                        low(f)
                else:
                    if nth < 4:
                        for f in range(KC):
                            low(f)
                    sum_up(KC - 1)
                dve.wait_ge(taken[0], FREE[f"norm{nth}"][0] + 2)
                V.reciprocal(rstd[:, :], total[:, :]).then_inc(rstd_made, 1)
                dve.wait_ge(rstd_made, nth + 1)

            H_BASE = {0: H_SC_IN, 1: H_FFN0, 2: H_QKV, 3: H_FFN1}

            def split_mixed(h_base):
                for f in range(KC):
                    dve.wait_ge(h_high, h_base + f + 1)
                    V.tensor_tensor(h_lo[:, f, :], mixed[:, f, :], h_hi[:, f, :].bitcast(f32),
                                    ALU.subtract).then_inc(h_ready, 1)

            def conv(m, par, tap):
                e, o = ext[par], y[par]
                V.tensor_scalar(o[:, 0:SEQ], e[:, 0:SEQ], tap(0), None, ALU.mult).then_inc(tapped, 1)
                dve.wait_ge(smp_full, m * 4 + 2)
                q, r = smp[par], y[par][:, SEQ:T].rearrange("p (b t) -> p b t", t=NT)
                V.tensor_scalar(r, q[:, :, 0:NT], tap(0), None, ALU.mult).then_inc(tapped, 1)
                for n in range(1, CW):
                    dve.wait_ge(tapped, m * 4 + (2 * n - 1))
                    main = V.scalar_tensor_tensor(o[:, 0:SEQ], e[:, n:n + SEQ], tap(n), o[:, 0:SEQ], ALU.mult, ALU.add)
                    if n < CW - 1:
                        main.then_inc(tapped, 1)
                    dve.wait_ge(tapped, m * 4 + 2 * n)
                    if n == CW - 1:
                        dve.wait_ge(smp_full, m * 4 + 4)
                    last = V.scalar_tensor_tensor(r, q[:, :, n:n + NT], tap(n), r, ALU.mult, ALU.add)
                    if n < CW - 1:
                        last.then_inc(tapped, 1)
                last.then_inc(convolved, 1)

            def ffn_chunk(m, par, chunk, layer, k, trip, slot):
                name = f"ffn{layer}"
                s = (k + 1) % 2
                dve.wait_ge(convolved, m + 1)
                dve.wait_ge(full[s], trip * TRIP_FILLS + (FULL[name][s] + k // 2 + 1))
                V.tensor_tensor(wide(ext[par][:, CW - 1:]), result(s), wide(rstd[:, :]), ALU.mult).then_inc(taken[s], 1)
                dve.wait_ge(taken[s], trip * TRIP_FILLS + (FREE[name][s] + k // 2 + 2))
                dve.wait_ge(a_ready, m - (KC - 1))
                conv(m, par, lambda t: tap_ffn[:, ds(chunk + layer * FC, 1), t:t + 1].rearrange("p o t -> p (o t)"))
                s = (k + 2) % 2
                dve.wait_ge(silued, m - (KC - 1))
                V.tensor_tensor(y[par][:, :], y[par][:, :], rstd[:, :], ALU.mult).then_inc(y_scaled, 1)
                dve.wait_ge(y_scaled, m + 1)
                dve.wait_ge(full[s], trip * TRIP_FILLS + (FULL[name][s] + (k + 1) // 2 + 1))
                yy = wide(y[par][:, :])
                V.tensor_tensor(yy, yy, result(s), ALU.mult).then_inc(taken[s], 1)
                dve.wait_ge(a_high, m - (KC - 1))
                V.tensor_tensor(a_lo[:, slot, par, :], y[par][:, :], a_hi[:, slot, par, :].bitcast(f32),
                                ALU.subtract).then_inc(a_ready, 1)

            def add_x(f, name, k, trip):
                s = (k + 1) % 2
                dve.wait_ge(full[s], trip * TRIP_FILLS + (FULL[name][s] + k // 2 + 1))
                xx = x[:, f, :].rearrange("p (a b) -> p a b", a=TJ)
                V.tensor_tensor(xx, xx, result(s), ALU.add).then_inc(taken[s], 1)

            def ffn(layer):
                name = f"ffn{layer}"
                m0 = M_FFN[layer]

                def up(m, chunk, k0, trip, slot):
                    for p in range(2):
                        ffn_chunk(m + p, p, chunk + p, layer, k0 + 2 * p, trip, slot)

                def down(k0, trip):
                    for f in range(KC):
                        add_x(f, name, k0 + f, trip)

                up(m0, 0, 0, 0, 0)
                with dve.Fori(0, FFN_TRIPS) as i:
                    for n in range(2):
                        k0 = (4 + KC) * n + 4
                        up(i * 4 + (m0 + 2 + 2 * n), i * 4 + (2 + 2 * n), k0, i, (n + 1) % 2)
                        down(k0 + 4, i)
                return lambda f: add_x(f, name, FFN_OUT - KC + f, 0)

            dve.wait_ge(gain_loaded, 16)
            norm(0, lambda f: dve.wait_ge(x_loaded[f], 16), True)
            dve.wait_ge(consts, 16 * 8)
            dve.wait_ge(made, 4)
            V.tensor_tensor(rstd2[:, :], rstd[:, :], rstd[:, :], ALU.mult).then_inc(squared_rstd, 1)
            dve.wait_ge(squared_rstd, 1)
            with dve.Fori(0, KC // 2) as i:
                for n in range(2):
                    m = i * 2 + n
                    k = 3 * n + 1
                    s = (k + 1) % 2
                    dve.wait_ge(convolved, m + 1)
                    gate = (k + 2) % 2
                    dve.wait_ge(taken[gate], i * 3 + (FREE["sc_in"][gate] + (k - 1) // 2 + 2))
                    V.tensor_tensor(c_gate[n][:, :], c_gate[n][:, :], rstd2[:, :], ALU.mult).then_inc(c_scaled, 1)
                    dve.wait_ge(c_scaled, m + 1)
                    dve.wait_ge(full[s], i * 3 + (FULL["sc_in"][s] + k // 2 + 1))
                    V.tensor_tensor(ext[n][:, CW - 1:].rearrange("p (a b) -> p a b", a=TJ),
                                    c_gate[n][:, :].rearrange("p (a b) -> p a b", a=TJ), result(s),
                                    ALU.mult).then_inc(taken[s], 1)
                    dve.wait_ge(taken[s], i * 3 + (FREE["sc_in"][s] + k // 2 + 2))
                    conv(m, n, lambda t: tap_sc[:, ds(m, 1), t:t + 1].rearrange("p o t -> p (o t)"))
                    k = 3 * n + 2
                    s = (k + 1) % 2
                    dve.wait_ge(convolved, m + 3)
                    V.tensor_tensor(y[n][:, :], y[n][:, :], rstd[:, :], ALU.mult).then_inc(y_scaled, 1)
                    dve.wait_ge(y_scaled, m + 1)
                    dve.wait_ge(full[s], i * 3 + (FULL["sc_in"][s] + k // 2 + 1))
                    V.tensor_tensor(mixed[:, ds(m, 1), :].rearrange("p o (a b) -> p (o a) b", a=TJ),
                                    y[n][:, :].rearrange("p (a b) -> p a b", a=TJ), result(s),
                                    ALU.mult).then_inc(taken[s], 1)
            split_mixed(H_SC_OUT)
            norm(1, lambda f: add_x(f, "sc_out", f, 0), False)
            last_add = ffn(0)
            norm(2, last_add, False)

            with dve.Fori(0, KC) as c:
                def take(dst, s, full_nth, scale=None):
                    dve.wait_ge(full[s], full_nth + 1)
                    if scale is None:
                        V.tensor_tensor(wide(dst[:, :]), result(s), wide(rstd[:, :]), ALU.mult).then_inc(taken[s], 1)
                    else:
                        V.scalar_tensor_tensor(wide(dst[:, :]), result(s), scale, wide(rstd[:, :]),
                                               ALU.mult, ALU.mult).then_inc(taken[s], 1)

                def copy_turned(u):
                    dve.wait_ge(turn_done, c * N_UNITS + (u + 1))
                    if u >= 2:
                        dve.wait_ge(pv_done, c * N_UNITS + (u - 1))
                    n = UNITS[u][2]
                    V.tensor_copy(w_t[u % 2][:, 0:n, :].rearrange("p a b -> p (a b)"),
                                  turned[u % 2][:, 0:n * P]).then_inc(w_t_by_dve, 1)

                def weigh(j):
                    i = STEPS[j][0]
                    width = P * (i + 1)
                    dve.wait_ge(beta_done, c * N_STEPS + (j + 1))
                    dve.wait_ge(keep_done, c * N_STEPS + (j + 3))
                    dve.wait_ge(weighed, c * N_STEPS + (j + 1))
                    back = keep[j % 2][:, width - 1:0:-1]
                    V.tensor_tensor_scan(prod[:, width - 1:0:-1], back, back, 1.0,
                                         ALU.mult, ALU.bypass).then_inc(scanned, 1)
                    dve.wait_ge(scanned, c * N_STEPS + (j + 3))
                    V.tensor_tensor(beta[j % 2][:, 0:width - 1], beta[j % 2][:, 0:width - 1], prod[:, 1:width],
                                    ALU.mult).then_inc(weighed, 1)

                dve.wait_ge(kv_free, c + 1)
                take(q_t, 0, c * 2 + FULL["qkv"][0], DH ** -0.5)
                take(k_t, 1, c + FULL["qkv"][1])
                weigh(0)
                weigh(1)
                take(v_t, 0, c * 2 + (FULL["qkv"][0] + 1))
                for u in range(N_UNITS):
                    if not BY_ACT[u]:
                        copy_turned(u)
                    j, first, _ = UNITS[u]
                    if u + 1 < N_UNITS and UNITS[u + 1][0] == j + 1 and j + 2 < N_STEPS:
                        weigh(j + 2)
                dve.wait_ge(pv_done, c * N_UNITS + N_UNITS)
                for s in (1, 0):
                    half = slice((1 - s) * (SEQ // 2), (2 - s) * (SEQ // 2))
                    V.tensor_copy(mixed[:, ds(c, 1), half].rearrange("p o t -> p (o t)"),
                                  attended[:, half]).then_inc(taken[s], 1)

            dve.wait_ge(kv_free, KC + 1)
            for n in range(2):
                V.memset(q_rows[n][:, :], 0.0).then_inc(made, 1)
            dve.wait_ge(made, 6)

            def sample_q(bp):
                if bp >= 2:
                    dve.wait_ge(s_scored, bp - 1)
                for h in range(2):
                    rows = slice(DH * h, DH * h + DH)
                    o = q_rows[bp % 2][rows, :].rearrange("p (c r) -> p c r", c=KC)[:, :, 0:P]
                    o = o.rearrange("p c (b r) -> p c b r", b=2)[:, :, :, h * NT:(h + 1) * NT]
                    q = q_s[rows, :, bp * 2 * NT:(bp + 1) * 2 * NT].rearrange("p c (b t) -> p c b t", b=2)
                    last = V.tensor_copy(o, q)
                last.then_inc(s_set, 1)

            def sample_weigh(bp):
                dve.wait_ge(s_beta, bp + 1)
                dve.wait_ge(s_keep, bp + 1)
                if bp:
                    dve.wait_ge(s_weighed, bp)
                n, w, back = PAST + NS, beta_s[bp % 2], keep_s[bp % 2][:, PAST + NS - 1:0:-1]
                V.tensor_tensor_scan(prod_s[:, n - 1:0:-1], back, back, 1.0, ALU.mult, ALU.bypass).then_inc(s_scan, 1)
                dve.wait_ge(s_scan, bp + 1)
                V.tensor_tensor(w[:, 0:n - 1], w[:, 0:n - 1], prod_s[:, 1:n], ALU.mult).then_inc(s_weighed, 1)

            def sample_copy(bp):
                dve.wait_ge(s_turned, bp + 1)
                V.tensor_copy(w_ts[:, 0:PAGES, :].rearrange("p a b -> p (a b)"), out[1][:, 2, 0:PAST])
                V.tensor_copy(w_ts[0:NS, PAGES, :], out[1][0:NS, 2, PAST:PAST + P]).then_inc(s_wt, 1)

            def sample_take(bp):
                dve.wait_ge(s_o_turned, bp + 1)
                for h in range(2):
                    rows = slice(DH * h, DH * h + DH)
                    o = mixed[rows, :, SEQ + bp * 2 * NT:SEQ + (bp + 1) * 2 * NT].rearrange("p c (b t) -> p c b t", b=2)
                    r = score[1][rows, :].rearrange("p (c b r) -> p c b r", c=KC, b=2)
                    for c in range(KC):
                        last = V.tensor_copy(o[:, c, :, :], r[:, c, :, 8 * c + 4 * h:8 * c + 4 * h + NT])
                last.then_inc(s_out, 1)

            sample_q(0)
            dve.wait_ge(s_vturned, 1)
            V.tensor_copy(v_new[:, :], score[1][0:NS, :]).then_inc(s_vnew, 1)
            sample_q(1)
            sample_weigh(0)
            for bp in range(NB // 2):
                sample_copy(bp)
                if bp + 2 < NB // 2:
                    sample_q(bp + 2)
                if bp + 1 < NB // 2:
                    sample_weigh(bp + 1)
                if bp:
                    sample_take(bp - 1)
            sample_take(NB // 2 - 1)
            for n in range(2):
                V.memset(ext[n][:, 0:CW - 1], 0.0).then_inc(made, 1)
            dve.wait_ge(made, 8)
            split_mixed(H_WO)
            norm(3, lambda f: add_x(f, "wo", f, 0), False)
            last_add = ffn(1)
            norm(4, last_add, False)
            for f in range(Y_BY_DVE):
                dve.wait_ge(y_gained, f + 1)
                V.tensor_tensor(y_rows[:, f, :], y_rows[:, f, :], rstd[:, :], ALU.mult).then_inc(y_made, 1)


def kernel(**inputs):
    import numpy as np
    import ml_dtypes
    import concourse.bacc as bacc
    from concourse.bass_utils import run_bass_kernel_spmd

    a = {k: np.asarray(v) for k, v in inputs.items()}

    def by_features(v):
        v = v.reshape(v.shape[:-1] + (v.shape[-1] // P, P))
        return np.moveaxis(np.moveaxis(v, -1, 0), -1, 1)

    def tiles(w, order):
        k, n = w.shape
        t = w.reshape(k // P, P, n // P, P).transpose(2, 1, 0, 3).reshape(n // P, P, k)
        return t[order]

    tokens = np.concatenate([a["x_prompt"].reshape(SEQ, D), a["x_sample"].reshape(NS, D)])
    chunks = np.arange(KC)
    sc_in = tiles(a["w_sc_in"][0], np.stack([KC + chunks, 2 * KC + chunks, chunks], 1).ravel())
    qkv = tiles(a["w_qkv"][0], np.stack([chunks, KC + chunks, 2 * KC + chunks], 1).ravel())

    def ffn(layer):
        hidden = np.arange(FC)
        up = tiles(a["w_ffn_up"][layer], np.stack([hidden, FC + hidden], 1).ravel())
        down = a["w_ffn_down"][layer].reshape(FC, P, D)
        rows = [up[0:4]]
        for g in range(1, PAIRS):
            rows += [up[4 * g:4 * g + 4], down[2 * g - 2:2 * g]]
        return rows + [down[FC - 2:]]

    weights = np.concatenate([sc_in, tiles(a["w_sc_out"][0], chunks), *ffn(0), qkv,
                              tiles(a["w_o"][0], chunks), *ffn(1)])
    gains = np.concatenate([np.stack([a["norm_mix"][0], a["norm_ffn"][0], a["norm_mix"][1], a["norm_ffn"][1],
                                      a["norm_final"]])])
    taps_sc = np.concatenate([a["w_sc_dw"][0], np.zeros((1, D), np.float32)])
    taps_ffn = np.concatenate([a["w_ffn_dw"], a["b_ffn_dw"][:, None, :]], 1)
    bf16 = ml_dtypes.bfloat16
    key, query = np.arange(P)[None, :], np.arange(P)[:, None]
    mask_diag = np.where(key < query, 0.0, MASKED).astype(bf16)
    row, new = np.arange(P)[:, None, None], np.arange(NS)[None, None, :]
    sample = 2 * np.arange(NB // 2)[None, :, None] + row // (P // 2)
    mask_new = np.where((new // NT == sample) & (new % NT < row % NT), 0.0, MASKED).astype(bf16)
    pool = a["cache_k"].shape[1]
    arrays = {
        "x_in": tokens.T.reshape(KC, P, T),
        "weights": weights,
        "taps_sc": by_features(taps_sc),
        "taps_ffn": by_features(taps_ffn).transpose(0, 2, 1, 3).reshape(P, 2 * FC, CW + 1),
        "state_sc": by_features(a["state_conv"][0]),
        "state_ffn": by_features(a["state_ffn"]).transpose(0, 2, 1, 3, 4).reshape(P, 2 * FC, NB, CW - 1),
        "gains": by_features(gains).transpose(0, 2, 1),
        "bias_heads": np.repeat(a["sb_bias"].reshape(1, H), P, 0),
        "bias_rows": np.tile(np.repeat(a["sb_bias"].reshape(H), NT), 2).reshape(P, 1),
        "cache_k": a["cache_k"][0].reshape(pool, PG, KC, P).transpose(0, 3, 2, 1),
        "cache_v": a["cache_v"][0].reshape(pool, PG, D),
        "pages": a["page_table"].reshape(1, NB * PAGES),
        "mask_diag": mask_diag,
        "mask_new": mask_new,
        "ident_in": np.eye(P, dtype=np.float32),
        "ident_b_in": np.eye(P, dtype=bf16),
    }
    arrays = {k: np.ascontiguousarray(v) for k, v in arrays.items()}
    outs = {"y_out": (KC, P, T), "k_out": (KC, P, T), "v_out": (KC, P, T),
            "conv_out": (P, KC, (1 + NB) * (CW - 1)), "ffn_out": (2, P, FC, (1 + NB) * (CW - 1))}
    nc = bacc.Bacc("TRN2", target_bir_lowering=False, num_devices=1, dynamic_dma_scratch_size=1024)
    args = {k: nc.dram_tensor(k, v.shape, mybir.dt.from_np(v.dtype), kind="ExternalInput").ap()
            for k, v in arrays.items()}
    args |= {k: nc.dram_tensor(k, shape, mybir.dt.float32, kind="ExternalOutput").ap() for k, shape in outs.items()}
    build(nc, **args)
    got = run_bass_kernel_spmd(nc, [arrays], core_ids=[0]).results[0]

    def by_tokens(v):
        v = v.reshape(D, T).T
        return v[:SEQ], v[SEQ:]

    y_p, y_s = by_tokens(got["y_out"])
    k_p, k_s = by_tokens(got["k_out"])
    v_p, v_s = by_tokens(got["v_out"])

    def states(v):
        v = v.transpose(2, 1, 0).reshape((1 + NB) * (CW - 1), -1)
        return v[:CW - 1], v[CW - 1:].reshape(NB, CW - 1, -1)

    conv_p, conv_s = states(got["conv_out"])
    ffn_p, ffn_s = zip(*(states(v) for v in got["ffn_out"]), strict=True)
    return (y_p.reshape(1, SEQ, D), y_s.reshape(NB, NT, D),
            k_p.reshape(1, 1, SEQ, H, DH), v_p.reshape(1, 1, SEQ, H, DH),
            conv_p[None, None], np.stack(ffn_p)[:, None],
            k_s.reshape(1, NB, NT, H, DH), v_s.reshape(1, NB, NT, H, DH),
            conv_s[None], np.stack(ffn_s))
```

```python
import concourse.bass as bass
from concourse import mybir
from contextlib import ExitStack

P = 128
D = 1024
KC = D // P
SEQ = 1024
NB, NT = 8, 4
NS = NB * NT
T = SEQ + NS
TJ = 3
TW = T // TJ
F = 2816
FC = F // P
CW = 3
H, DH = 16, 64
PAGES, PG = 2, 128
PAST = PAGES * PG
EPS = 1e-6
MASKED = -1e30

N_SC_IN, N_SC_OUT, N_FFN, N_QKV, N_WO = 3 * KC, KC, 3 * FC, 3 * KC, KC
T_SC_IN = 0
T_SC_OUT = T_SC_IN + N_SC_IN
T_FFN0 = T_SC_OUT + N_SC_OUT
T_QKV = T_FFN0 + N_FFN
T_WO = T_QKV + N_QKV
T_FFN1 = T_WO + N_WO
N_TILES = T_FFN1 + N_FFN
RAW, SPLIT = 2, 3
UNROLL = RAW * SPLIT

PAIRS = FC // 2
FFN_TRIPS = (PAIRS - 1) // 2
FFN_OUT = 4 * PAIRS + KC * PAIRS
TRIP_FILLS = 4 + KC

FULL = {}
FREE = {}


def _count():
    full, free = [0, 0], [0, 0]

    def phase(name, full0, full1, free0=None, free1=None):
        FULL[name] = tuple(full)
        FREE[name] = tuple(free)
        full[0] += full0
        full[1] += full1
        free[0] += full0 if free0 is None else free0
        free[1] += full1 if free1 is None else free1

    phase("norm0", 1, 0)
    phase("sc_in", N_SC_IN // 2, N_SC_IN // 2)
    phase("sc_out", KC // 2, KC // 2)
    phase("norm1", 1, 0)
    phase("ffn0", FFN_OUT // 2, FFN_OUT // 2)
    phase("norm2", 1, 0)
    phase("qkv", 2 * KC, KC, 3 * KC, 2 * KC)
    phase("wo", KC // 2, KC // 2)
    phase("norm3", 1, 0)
    phase("ffn1", FFN_OUT // 2, FFN_OUT // 2)
    phase("norm4", 1, 0)


_count()
M_FFN = (KC, KC + FC)
H_SC_IN, H_SC_OUT, H_FFN0, H_QKV, H_WO, H_FFN1 = (KC * n for n in range(6))
QT = SEQ // P
STEPS = [(i, h) for i in range(QT - 1, -1, -1) for h in range(2)]
UNITS = [(j, first, min(4, i + 1 - first)) for j, (i, h) in enumerate(STEPS) for first in range(0, i + 1, 4)]
BY_ACT = [STEPS[j][0] >= 4 and first == 0 for j, first, n in UNITS]
N_STEPS, N_UNITS = len(STEPS), len(UNITS)
W_T = 4
AHEAD = W_T - 1
Y_BY_DVE = 5


def copied(u):
    return BY_ACT[u], sum(a == BY_ACT[u] for a in BY_ACT[:u + 1])


def first_unit(j):
    return min(u for u in range(N_UNITS) if UNITS[u][0] == j)


def turned_by(j):
    return 1 + max(u for u in range(N_UNITS) if UNITS[u][0] == j)


def build(nc, x_in, weights, taps_sc, taps_ffn, state_sc, state_ffn, gains, bias_heads, bias_rows,
          cache_k, cache_v, pages, mask_diag, mask_new, ident_in, ident_b_in,
          y_out, k_out, v_out, conv_out, ffn_out):
    f32, f32r, bf16, i32 = mybir.dt.float32, mybir.dt.float32r, mybir.dt.bfloat16, mybir.dt.int32
    ACT, ALU = mybir.ActivationFunctionType, mybir.AluOpType
    ds = bass.ds
    ctx = ExitStack()
    with ctx:
        base = -(-nc.sbuf_base // 64) * 64
        arena = nc.sbuf_usable_end - base
        arena -= arena % 64
        ctx.enter_context(nc.sbuf_tensor("arena", [P, arena // 4], f32))
        top = [base]

        def at(offset, name, shape, dt):
            return nc.alloc_sbuf_tensor_at(name, shape, dt, offset=offset)

        def size(shape, dt):
            n = 1
            for d in shape[1:]:
                n *= d
            return -(-n * (2 if dt == bf16 else 4) // 32) * 32

        def sb(name, shape, dt=f32):
            t = at(top[0], name, shape, dt)
            top[0] += size(shape, dt)
            assert top[0] <= base + arena, name
            return t

        x = sb("x", [P, KC, T])
        h_at = top[0]
        h_hi = sb("h_hi", [P, KC, T], f32r)
        h_lo = sb("h_lo", [P, KC, T], f32r)
        h_end = top[0]
        raw = [sb(f"raw{n}", [P, D]) for n in range(RAW)]
        w_hi = [sb(f"w_hi{n}", [P, D], f32r) for n in range(SPLIT)]
        w_lo = [sb(f"w_lo{n}", [P, D], f32r) for n in range(SPLIT)]
        mean = sb("mean", [P, P])
        ident = sb("ident", [P, P])
        ident_b = sb("ident_b", [P, P], bf16)
        diag_b = sb("diag_b", [P, P], bf16)
        new_b = sb("new_b", [P, NB // 2, NS], bf16)
        gain = sb("gain", [P, 5, KC])
        tap_sc = sb("tap_sc", [P, KC, CW + 1])
        tap_ffn = sb("tap_ffn", [P, 2 * FC, CW + 1])
        st_sc = sb("st_sc", [P, KC, NB, CW - 1])
        st_ffn = sb("st_ffn", [P, 2 * FC, NB, CW - 1])
        new_sc = sb("new_sc", [P, KC, (1 + NB) * (CW - 1)])
        bias_h = sb("bias_h", [P, 2, H])
        bias_r = sb("bias_r", [P, 2])
        eps = sb("eps", [P, 1])
        bias_now = [sb(f"bias_now{n}", [P, 1]) for n in range(2)]
        bias_pair = sb("bias_pair", [P, 2, 2])
        page_row = sb("page_row", [1, NB * PAGES], i32)
        rstd = sb("rstd", [P, T])
        overlay = top[0]
        mixed = sb("mixed", [P, KC, T])
        after_mixed = top[0]
        ext = [sb(f"ext{n}", [P, T + CW - 1]) for n in range(2)]
        smp = [sb(f"smp{n}", [P, NB, CW - 1 + NT]) for n in range(2)]
        y = [sb(f"y{n}", [P, T]) for n in range(2)]
        square = [sb(f"square{n}", [P, T]) for n in range(2)]
        total = sb("total", [P, T])
        c_gate = [sb(f"c_gate{n}", [P, T]) for n in range(2)]
        new_ffn = sb("new_ffn", [P, FC, (1 + NB) * (CW - 1)])
        rstd2 = total
        top[0] = overlay
        a_hi = sb("a_hi", [P, 2, 2, T], f32r)
        a_lo = sb("a_lo", [P, 2, 2, T], f32r)
        assert top[0] == after_mixed
        q_t = sb("q_t", [P, T])
        k_t = sb("k_t", [P, T])
        v_t = sb("v_t", [P, T])
        v_rows = sb("v_rows", [P, QT, P])
        q_s = sb("q_s", [P, KC, NS])
        k_s = sb("k_s", [P, KC, NS])
        v_s = sb("v_s", [P, KC, NS])
        after_s = top[0]
        beta = [sb(f"beta{n}", [P, SEQ]) for n in range(2)]
        keep = [sb(f"keep{n}", [P, SEQ]) for n in range(2)]
        prod = sb("prod", [P, SEQ])
        w_t = [sb(f"w_t{n}", [P, 4, P]) for n in range(W_T)]
        top[0] = h_at
        page_k = [sb(f"page_k{n}", [P, KC, PAGES, PG]) for n in range(4)]
        page_v = [sb(f"page_v{n}", [P, PAGES, D]) for n in range(4)]
        assert top[0] <= h_end
        top[0] = after_mixed
        q_rows = [sb(f"q_rows{n}", [P, KC * (P + 2 * NT)]) for n in range(2)]
        assert top[0] <= after_s - 3 * size(q_s.shape, f32)
        top[0] = after_s
        v_new = sb("v_new", [NS, D])
        o_rows = sb("o_rows", [P, D])
        beta_s = [sb(f"beta_s{n}", [P, PAST + NS]) for n in range(2)]
        keep_s = [sb(f"keep_s{n}", [P, PAST + NS]) for n in range(2)]
        prod_s = sb("prod_s", [P, PAST + NS])
        w_ts = sb("w_ts", [P, PAGES + 1, P])
        y_rows = at(h_at, "y_rows", [P, KC, T], f32)

        bank = [ctx.enter_context(nc.psum_tensor(f"bank{n}", [P, 3 if n < 2 else 2, 512], f32)) for n in range(3)]
        out = [bank[0], bank[1]]
        spare = bank[2]

        def result(s):
            return out[s][:, :, 0:TW]

        score = [out[1][:, 0:2, :].rearrange("p a b -> p (a b)"), spare[:, :, :].rearrange("p a b -> p (a b)")]
        turned = [out[1][:, 2, :], out[0][:, 2, :]]
        attended = out[0][:, 0:2, :].rearrange("p a b -> p (a b)")

        def sem(name):
            return ctx.enter_context(nc.semaphore(name))

        raw_loaded = [sem(f"raw_loaded{n}") for n in range(RAW)]
        w_high = sem("w_high")
        w_split = sem("w_split")
        w_used = sem("w_used")
        full = [sem("full0"), sem("full1")]
        taken = [sem("taken0"), sem("taken1")]
        x_loaded = [sem(f"x_loaded{f}") for f in range(KC)]
        gain_loaded = sem("gain_loaded")
        squared_rstd = sem("squared_rstd")
        c_scaled = sem("c_scaled")
        y_scaled = sem("y_scaled")
        s_o_rows = sem("s_o_rows")
        s_o_turned = sem("s_o_turned")
        y_gained = sem("y_gained")
        y_by_pool = sem("y_by_pool")
        root_made = sem("root_made")
        consts = sem("consts")
        state_loaded = sem("state_loaded")
        made = sem("made")
        kv_free = sem("kv_free")
        negated = sem("negated")
        rstd_made = sem("rstd_made")
        bias_set = sem("bias_set")
        pair_bias_set = sem("pair_bias_set")
        split_begun = sem("split_begun")
        new_copied = sem("new_copied")
        squared = sem("squared")
        summed = sem("summed")
        h_high = sem("h_high")
        h_ready = sem("h_ready")
        smp_full = sem("smp_full")
        tapped = sem("tapped")
        convolved = sem("convolved")
        silued = sem("silued")
        a_high = sem("a_high")
        a_ready = sem("a_ready")
        kv_stored = sem("kv_stored")
        v_turned = sem("v_turned")
        v_ready = sem("v_ready")
        scored = sem("scored")
        beta_done = sem("beta_done")
        keep_done = sem("keep_done")
        scanned = sem("scanned")
        weighed = sem("weighed")
        turn_done = sem("turn_done")
        w_t_by_act = sem("w_t_by_act")
        w_t_by_dve = sem("w_t_by_dve")
        pv_done = sem("pv_done")
        page_k_in = [sem(f"page_k_in{n}") for n in range(4)]
        page_v_in = [sem(f"page_v_in{n}") for n in range(4)]
        page_ids = sem("page_ids")
        s_set = sem("s_set")
        s_scored = sem("s_scored")
        s_beta = sem("s_beta")
        s_keep = sem("s_keep")
        s_scan = sem("s_scan")
        s_weighed = sem("s_weighed")
        s_turned = sem("s_turned")
        s_wt = sem("s_wt")
        s_full = sem("s_full")
        s_vturned = sem("s_vturned")
        s_vnew = sem("s_vnew")
        s_out = sem("s_out")
        y_made = sem("y_made")
        stored = sem("stored")

        block = ctx.enter_context(nc.Block())

        @block.sync
        def _(sp):
            def load_tile(n, slot):
                sp.wait_ge(w_split, n + 1)
                sp.dma_start(raw[slot][:, :], weights[ds(n, 1), :, :].rearrange("o p n -> p (o n)")).then_inc(raw_loaded[slot], 16)

            sp.sem_inc(w_split, RAW)
            sp.sem_inc(s_scored, 2)
            sp.sem_inc(s_full, 2)
            load_tile(0, 0)
            for f in range(1, KC, 2):
                sp.dma_start(x[:, f, :], x_in[f, :, :]).then_inc(x_loaded[f], 16)
            load_tile(1, 1)
            sp.dma_start(tap_sc[:, :, :], taps_sc).then_inc(consts, 16)
            sp.dma_start(st_sc[:, :, :, :], state_sc).then_inc(state_loaded, 16)
            sp.dma_start(page_row[:, :], pages).then_inc(page_ids, 16)
            sp.dma_start(tap_ffn[:, :, :], taps_ffn).then_inc(consts, 16)
            sp.dma_start(ident[:, :], ident_in).then_inc(consts, 16)
            sp.dma_start(ident_b[:, :], ident_b_in).then_inc(consts, 16)
            sp.dma_start(diag_b[:, :], mask_diag).then_inc(consts, 16)
            for n in range(2, UNROLL):
                load_tile(n, n % RAW)
            sp.dma_start(new_b[:, :, :], mask_new).then_inc(consts, 16)
            sp.dma_start(bias_h[:, 0, :], bias_heads).then_inc(consts, 16)
            sp.dma_start(bias_r[:, 0:1], bias_rows).then_inc(consts, 16)
            sp.dma_start(st_ffn[:, :, :, :], state_ffn).then_inc(state_loaded, 16)
            early = T_WO + SPLIT + 1
            assert early % UNROLL == 0
            with sp.Fori(1, early // UNROLL) as i:
                for u in range(UNROLL):
                    load_tile(i * UNROLL + u, u % RAW)
            sp.wait_ge(page_ids, 16)
            sp.wait_ge(taken[0], FREE["qkv"][0] + 3 * (KC - 1) + 2 + 1)
            with sp.Fori(0, 2) as i:
                for pair in range(2):
                    def page(n, g):
                        return sp.value_load(page_row[0:1, ds(i * 8 + n * PAGES + g, 1)],
                                             min_val=0, max_val=cache_k.shape[0] - 1)

                    ids = [page(n, g) for n in (2 * pair, 2 * pair + 1) for g in range(PAGES)]
                    sp.wait_ge(s_scored, i * 2 + (pair + 1))
                    for n in (2 * pair, 2 * pair + 1):
                        for g in range(PAGES):
                            sp.dma_start(page_k[n][:, :, g, :],
                                         cache_k[ds(ids[n % 2 * PAGES + g], 1), :, :, :].rearrange("o p c t -> p (o c) t")).then_inc(page_k_in[n], 16)
                    sp.wait_ge(s_full, i * 2 + (pair + 1))
                    for n in (2 * pair, 2 * pair + 1):
                        for g in range(PAGES):
                            sp.dma_start(page_v[n][:, g, :],
                                         cache_v[ds(ids[n % 2 * PAGES + g], 1), :, :].rearrange("o p n -> p (o n)")).then_inc(page_v_in[n], 16)
            rest = N_TILES - early
            with sp.Fori(0, rest // UNROLL) as i:
                for u in range(UNROLL):
                    load_tile(i * UNROLL + (early + u), u % RAW)
            for n in range(rest - rest % UNROLL, rest):
                load_tile(early + n, n % RAW)

        @block.gpsimd
        def _(pool):
            def split_tile(n, slot, ring, nth):
                pool.wait_ge(raw_loaded[slot], nth * 16)
                pool.wait_ge(w_used, n + 1)
                pool.sem_inc(split_begun, 1)
                nc.gpsimd.tensor_copy(w_hi[ring][:, :], raw[slot][:, :]).then_inc(w_high, 1)
                pool.wait_ge(w_high, n + 1)
                nc.gpsimd.tensor_tensor(w_lo[ring][:, :], raw[slot][:, :], w_hi[ring][:, :].bitcast(f32),
                                        ALU.subtract).then_inc(w_split, 1)

            pool.sem_inc(w_used, SPLIT - 1)
            with pool.Fori(0, N_TILES // UNROLL) as i:
                for u in range(UNROLL):
                    split_tile(i * UNROLL + u, u % RAW, u % SPLIT, i * (UNROLL // RAW) + (u // RAW + 1))
            for n in range(N_TILES - N_TILES % UNROLL, N_TILES):
                split_tile(n, n % RAW, n % SPLIT, n // RAW + 1)
            for j in range(TJ):
                block = slice(j * TW, (j + 1) * TW)
                pool.wait_ge(rstd_made, 4 + j + 1)
                for f in range(Y_BY_DVE, KC):
                    if j == 0:
                        pool.wait_ge(y_gained, f + 1)
                    nc.gpsimd.tensor_tensor(y_rows[:, f, block], y_rows[:, f, block], rstd[:, block],
                                            ALU.mult).then_inc(y_by_pool, 1)

        @block.tensor
        def _(pe):
            def three(o, w, c0, hi, lo, first, last, counts=False):
                mm = nc.tensor.matmul(o, w_hi[w][:, c0:c0 + P], hi, start=first, stop=False)
                if counts:
                    mm.then_inc(w_used, 1)
                nc.tensor.matmul(o, w_hi[w][:, c0:c0 + P], lo, start=False, stop=False)
                return nc.tensor.matmul(o, w_lo[w][:, c0:c0 + P], hi, start=False, stop=last)

            def norm_sum(name, nth):
                pe.wait_ge(summed, KC * (nth + 1))
                pe.wait_ge(taken[0], FREE[name][0] + 1)
                for j in range(TJ):
                    mm = nc.tensor.matmul(out[0][:, j, 0:TW], mean[:, :], total[:, j * TW:(j + 1) * TW],
                                          start=True, stop=True)
                mm.then_inc(full[0], 1)

            def linear(tile, ring, s, fill, h_base=None, midway=None):
                pe.wait_ge(w_split, tile + (RAW + 1))
                pe.wait_ge(taken[s], fill + 1)
                for k in range(KC):
                    if h_base is not None:
                        pe.wait_ge(h_ready, h_base + k + 1)
                    for j in range(TJ):
                        mm = three(out[s][:, j, 0:TW], ring, k * P, h_hi[:, k, j * TW:(j + 1) * TW],
                                   h_lo[:, k, j * TW:(j + 1) * TW], k == 0, k == KC - 1,
                                   k == j == 0)
                    if k == 2 and midway is not None:
                        midway()
                mm.then_inc(full[s], 1)

            def tiles_of(name, tile0, h_base):
                for k in range(KC):
                    s = (k + 1) % 2
                    linear(tile0 + k, (tile0 + k) % SPLIT, s, FREE[name][s] + k // 2,
                           h_base if k == 0 else None)

            def up(tile, ring0, k0, name, trip, h_base=None, norm=None):
                for n in range(4):
                    s = (k0 + n + 1) % 2
                    linear(tile + n, (ring0 + n) % SPLIT, s, trip * TRIP_FILLS + (FREE[name][s] + (k0 + n) // 2),
                           h_base if n == 0 else None)
                    if n == 0 and norm is not None:
                        norm_sum(f"norm{norm}", norm)

            def down(tile, ring0, k0, name, trip, slot, group, early_release):
                order = [(f, kk) for f in range(KC) for kk in range(2)]
                if early_release:
                    order[-4:] = [(KC - 2, 0), (KC - 1, 0), (KC - 2, 1), (KC - 1, 1)]
                release = (KC - 2, 1) if early_release else (KC - 1, 1)
                for f, kk in order:
                    s = (k0 + f + 1) % 2
                    if f == 0:
                        pe.wait_ge(w_split, tile + (RAW + 1 + kk))
                        pe.wait_ge(a_ready, group * 2 + (3 + kk))
                    if kk == 0:
                        pe.wait_ge(taken[s], trip * TRIP_FILLS + (FREE[name][s] + (k0 + f) // 2 + 1))
                    for j in range(TJ):
                        mm = three(out[s][:, j, 0:TW], (ring0 + kk) % SPLIT, f * P,
                                   a_hi[:, slot, kk, j * TW:(j + 1) * TW],
                                   a_lo[:, slot, kk, j * TW:(j + 1) * TW], kk == 0, kk == 1,
                                   j == 0 and (f, kk) in (order[0], release))
                    if kk == 1:
                        mm.then_inc(full[s], 1)

            def ffn(layer):
                name = f"ffn{layer}"
                t0 = (T_FFN0, T_FFN1)[layer]
                g0 = layer * PAIRS
                up(t0, t0, 0, name, 0, (H_FFN0, H_FFN1)[layer], (1, 3)[layer])
                with pe.Fori(0, FFN_TRIPS) as i:
                    for n in range(2):
                        r0 = t0 + 4 + 6 * n
                        k0 = 4 + (4 + KC) * n
                        up(i * 12 + r0, r0, k0, name, i)
                        down(i * 12 + (r0 + 4), r0 + 4, k0 + 4, name, i, n, i * 2 + (g0 + n), n == 1)
                last = 4 + 6 * (PAIRS - 1)
                down(t0 + last, t0 + last, 4 + (4 + KC) * (PAIRS - 1), name, 0, 0, g0 + PAIRS - 1, False)

            pe.wait_ge(made, 1)

            def sc_in(trip, first):
                for n in range(6):
                    s = (n + 1) % 2
                    linear(trip * 6 + n, n % SPLIT, s, trip * 3 + (FREE["sc_in"][s] + n // 2),
                           H_SC_IN if first and n == 0 else None)
                    if first and n == 0:
                        norm_sum("norm0", 0)

            sc_in(0, True)
            with pe.Fori(1, KC // 2) as i:
                sc_in(i, False)
            tiles_of("sc_out", T_SC_OUT, H_SC_OUT)
            ffn(0)

            def scores(pair, j):
                i, h = STEPS[j]
                rows = slice(DH * h, DH * h + DH)
                pe.wait_ge(keep_done, pair * N_STEPS + (j + 1))
                width = P * (i + 1)
                for n0 in range(0, width, 512):
                    n1 = min(n0 + 512, width)
                    nc.tensor.matmul(score[j % 2][:, n0:n1], q_t[rows, i * P:(i + 1) * P], k_t[rows, n0:n1],
                                     start=True, stop=n1 < width)
                nc.tensor.matmul(score[j % 2][:, width - P:width], ident_b[:, :], diag_b[:, :],
                                 start=False, stop=True).then_inc(scored, 1)

            def unit_copied(pair, u):
                by_act, n = copied(u)
                if by_act:
                    pe.wait_ge(w_t_by_act, pair * sum(BY_ACT) + n)
                else:
                    pe.wait_ge(w_t_by_dve, pair * (N_UNITS - sum(BY_ACT)) + n)

            def turn(pair, u):
                j, first, n = UNITS[u]
                pe.wait_ge(weighed, pair * N_STEPS + (j + 2))
                if u >= 2:
                    unit_copied(pair, u - 2)
                for b in range(n):
                    mm = nc.tensor.transpose(turned[u % 2][:, b * P:(b + 1) * P],
                                             beta[j % 2][:, (first + b) * P:(first + b + 1) * P], ident[:, :])
                mm.then_inc(turn_done, 1)

            def values(pair, u):
                j, first, n = UNITS[u]
                i, h = STEPS[j]
                unit_copied(pair, u)
                for b in range(n):
                    mm = nc.tensor.matmul(attended[DH * h:DH * h + DH, i * P:(i + 1) * P],
                                          v_rows[:, first + b, DH * h:DH * h + DH], w_t[u % W_T][:, b, :],
                                          start=first + b == 0, stop=first + b == i)
                mm.then_inc(pv_done, 1)

            norm_sum("norm2", 2)
            with pe.Fori(0, KC) as c:
                tile = c * 3 + T_QKV
                f0 = c * 3 + FREE["qkv"][0]
                f1 = c * 2 + FREE["qkv"][1]

                def first_scores():
                    pe.wait_ge(taken[0], f0 + 2)
                    pe.wait_ge(taken[1], f1 + 2)
                    scores(c, 0)
                    scores(c, 1)

                pe.wait_ge(taken[1], f1 + 1)
                linear(tile, T_QKV % SPLIT, 0, f0, H_QKV)
                linear(tile + 1, (T_QKV + 1) % SPLIT, 1, f1)
                linear(tile + 2, (T_QKV + 2) % SPLIT, 0, f0 + 1, None, first_scores)
                for u in range(-AHEAD, N_UNITS):
                    ahead = u + AHEAD
                    if ahead < N_UNITS:
                        j, first, _ = UNITS[ahead]
                        if first == 0 and j + 2 < N_STEPS:
                            scores(c, j + 2)
                        turn(c, ahead)
                    if u == -AHEAD:
                        pe.wait_ge(taken[0], f0 + 3)
                        for b in range(QT):
                            mm = nc.tensor.transpose(attended[:, b * P:(b + 1) * P],
                                                     v_t[:, b * P:(b + 1) * P], ident[:, :])
                        mm.then_inc(v_turned, 1)
                    if u == 0:
                        pe.wait_ge(v_ready, c + 1)
                    if u >= 0:
                        values(c, u)

            pe.wait_ge(taken[0], FREE["wo"][0] + 1)
            pe.wait_ge(taken[1], FREE["wo"][1] + 1)
            for c in range(KC):
                mm = nc.tensor.transpose(score[1][0:NS, c * P:(c + 1) * P], v_s[:, c, :], ident[:, :])
            mm.then_inc(s_vturned, 1)

            def sample_scores(bp):
                pe.wait_ge(s_set, bp + 1)
                bank_s = out[1][:, bp % 2, :]
                for b in range(2):
                    slot, rows = 2 * (bp % 2) + b, slice(64 * b, 64 * b + 64)
                    pe.wait_ge(page_k_in[slot], (bp // 2 + 1) * 32)
                    for c in range(KC):
                        nc.tensor.matmul(bank_s[rows, 0:PAST], q_rows[bp % 2][:, c * P + 64 * b:c * P + 64 * b + 64],
                                         page_k[slot][:, c, :, :].rearrange("p g t -> p (g t)"),
                                         start=c == 0, stop=c == KC - 1, skip_group_check=True)
                for c in range(KC):
                    nc.tensor.matmul(bank_s[:, PAST:PAST + NS], q_rows[bp % 2][:, c * P:(c + 1) * P], k_s[:, c, :],
                                     start=c == 0, stop=False, skip_group_check=True)
                nc.tensor.matmul(bank_s[:, PAST:PAST + NS], ident_b[:, :], new_b[:, bp, :], start=False,
                                 stop=True, skip_group_check=True).then_inc(s_scored, 1)

            def sample_turn(bp):
                pe.wait_ge(s_weighed, bp + 1)
                w = beta_s[bp % 2]
                for g in range(PAGES):
                    nc.tensor.transpose(out[1][:, 2, g * P:(g + 1) * P], w[:, g * P:(g + 1) * P], ident[:, :])
                nc.tensor.transpose(out[1][0:NS, 2, PAST:PAST + P], w[:, PAST:PAST + NS],
                                    ident[:, :]).then_inc(s_turned, 1)

            def sample_values(bp):
                pe.wait_ge(s_wt, bp + 1)
                if bp:
                    pe.wait_ge(s_o_rows, bp)
                for half in range(2):
                    nc.tensor.matmul(out[0][:, half, :], w_ts[0:NS, PAGES, :], v_new[:, 512 * half:512 * half + 512],
                                     start=True, stop=False, skip_group_check=True)
                for b in range(2):
                    slot, rows = 2 * (bp % 2) + b, slice(64 * b, 64 * b + 64)
                    pe.wait_ge(page_v_in[slot], (bp // 2 + 1) * 32)
                    for half in range(2):
                        for g in range(PAGES):
                            mm = nc.tensor.matmul(out[0][rows, half, :], w_ts[:, g, rows],
                                                  page_v[slot][:, g, 512 * half:512 * half + 512], start=False,
                                                  stop=g == PAGES - 1, skip_group_check=True)
                mm.then_inc(s_full, 1)

            def sample_out(bp):
                pe.wait_ge(s_o_rows, bp + 1)
                pe.wait_ge(s_out, bp + 1)
                for c in range(KC):
                    mm = nc.tensor.transpose(score[1][:, c * P:(c + 1) * P], o_rows[:, c * P:(c + 1) * P], ident[:, :])
                mm.then_inc(s_o_turned, 1)

            sample_scores(0)
            pe.wait_ge(s_vnew, 1)
            for bp in range(NB // 2):
                if bp + 1 < NB // 2:
                    sample_scores(bp + 1)
                if bp:
                    sample_out(bp - 1)
                sample_turn(bp)
                sample_values(bp)
            sample_out(NB // 2 - 1)
            pe.wait_ge(s_out, NB // 2 + 1)
            tiles_of("wo", T_WO, H_WO)
            ffn(1)
            norm_sum("norm4", 4)

        @block.scalar
        def _(act):
            def act_op(o, i, func=ACT.Copy, **kw):
                return nc.scalar.activation(o, i, func, **kw)

            act.dma_start(gain[:, :, :], gains).then_inc(gain_loaded, 16)
            for f in range(0, KC, 2):
                act.dma_start(x[:, f, :], x_in[f, :, :]).then_inc(x_loaded[f], 16)
            act.sem_inc(convolved, 2)

            def norm(nth, layer_before, k_before, h_first):
                act.preload_act_table(ACT.Sqrt)

                def ready(f):
                    if nth == 0:
                        act.wait_ge(x_loaded[f], 16)
                    else:
                        k = k_before + f
                        s = (k + 1) % 2
                        act.wait_ge(taken[s], FREE[layer_before][s] + k // 2 + 2)

                def high(f):
                    act_op(h_hi[:, f, :], x[:, f, :], scale=gain[:, nth, f:f + 1]).then_inc(h_high, 1)

                def gained(f):
                    act_op(y_rows[:, f, :], x[:, f, :], scale=gain[:, nth, f:f + 1]).then_inc(y_gained, 1)

                def root():
                    act.wait_ge(full[0], FULL[f"norm{nth}"][0] + 1)
                    act_op(total[:, :].rearrange("p (a b) -> p a b", a=TJ), result(0), ACT.Sqrt,
                           bias=eps[:, 0:1]).then_inc(taken[0], 1)

                def square_of(f):
                    if f >= 2:
                        act.wait_ge(summed, KC * nth + f - 1)
                    act_op(square[f % 2][:, :], x[:, f, :], ACT.Square).then_inc(squared, 1)

                for f in range(KC):
                    if nth in (1, 3) and f == KC - 1:
                        s = (k_before + f + 1) % 2
                        act.wait_ge(full[s], FULL[layer_before][s] + (k_before + f) // 2 + 1)
                        for g in range(KC - 1):
                            high(g)
                    ready(f)
                    if nth == 4 or (not h_first and f < KC - 1):
                        square_of(f)
                        if nth == 4 and f < KC - 1:
                            gained(f)
                    elif h_first:
                        high(f)
                if h_first:
                    for f in range(KC):
                        square_of(f)
                elif nth == 2:
                    square_of(KC - 1)
                    for f in range(3):
                        high(f)
                    root()
                    for f in range(3, KC):
                        high(f)
                elif nth < 4:
                    high(KC - 1)
                    square_of(KC - 1)
                if nth == 4:
                    gained(KC - 1)
                if nth == 4:
                    act.wait_ge(full[0], FULL["norm4"][0] + 1)
                    for j in range(TJ):
                        act_op(total[:, j * TW:(j + 1) * TW], out[0][:, j, 0:TW], ACT.Sqrt,
                               bias=eps[:, 0:1]).then_inc(root_made, 1)
                elif nth != 2:
                    root()

            def split_mixed(before_last=None):
                for f in range(KC):
                    if f == KC - 1 and before_last is not None:
                        before_last()
                    act_op(h_hi[:, f, :], mixed[:, f, :]).then_inc(h_high, 1)

            def samples(m, par, states, kept):
                tokens = ext[par][:, CW - 1 + SEQ:CW - 1 + T].rearrange("p (b t) -> p b t", t=NT)
                act_op(smp[par][:, :, CW - 1:], tokens).then_inc(smp_full, 1)
                act_op(smp[par][:, :, 0:CW - 1], states).then_inc(smp_full, 1)
                act_op(kept[:, 0:CW - 1], ext[par][:, SEQ:SEQ + CW - 1]).then_inc(smp_full, 1)
                act_op(kept[:, CW - 1:].rearrange("p (b t) -> p b t", t=CW - 1),
                       tokens[:, :, NT - CW + 1:]).then_inc(smp_full, 1)

            def ffn_chunk(m, par, chunk, layer, k, trip, slot, group):
                name = f"ffn{layer}"
                s = (k + 1) % 2
                act.wait_ge(taken[s], trip * TRIP_FILLS + (FREE[name][s] + k // 2 + 2))
                samples(m, par, st_ffn[:, ds(chunk + layer * FC, 1), :, :].rearrange("p o b t -> p (o b) t"),
                        new_ffn[:, ds(chunk, 1), :].rearrange("p o t -> p (o t)"))
                act_op(bias_now[par][:, :], tap_ffn[:, ds(chunk + layer * FC, 1), CW:CW + 1].rearrange("p o t -> p (o t)")
                       ).then_inc(bias_set, 1)
                act.wait_ge(bias_set, m - (KC - 1))
                act.wait_ge(convolved, m + 3)
                act_op(y[par][:, :], y[par][:, :], ACT.Silu, bias=bias_now[par][:, :]).then_inc(silued, 1)
                s = (k + 2) % 2
                act.wait_ge(taken[s], trip * TRIP_FILLS + (FREE[name][s] + (k + 1) // 2 + 2))
                if par == 0 and group is not None:
                    act.wait_ge(taken[0], group)
                act_op(a_hi[:, slot, par, :], y[par][:, :]).then_inc(a_high, 1)

            def ffn(layer):
                name = f"ffn{layer}"
                m0 = M_FFN[layer]
                for p in range(2):
                    ffn_chunk(m0 + p, p, p, layer, 2 * p, 0, 0, None)
                with act.Fori(0, FFN_TRIPS) as i:
                    for n in range(2):
                        k0 = (4 + KC) * n + 4
                        for p in range(2):
                            ffn_chunk(i * 4 + (m0 + 2 + 2 * n + p), p, i * 4 + (2 + 2 * n + p), layer,
                                      k0 + 2 * p, i, (n + 1) % 2, i * TRIP_FILLS + (FREE[name][0] + (k0 - 1) // 2 + 2))
                act.wait_ge(smp_full, 4 * (m0 + FC))
                act.dma_start(ffn_out[layer], new_ffn[:, :, :]).then_inc(stored, 16)

            act.wait_ge(gain_loaded, 16)
            act.wait_ge(made, 2)
            norm(0, None, 0, True)
            act.wait_ge(state_loaded, 32)
            act.wait_ge(consts, 16 * 8)
            act_op(bias_h[:, 1, :], bias_h[:, 0, :], scale=-1.0).then_inc(negated, 1)
            act_op(bias_r[:, 1:2], bias_r[:, 0:1], scale=-1.0).then_inc(negated, 1)
            with act.Fori(0, KC // 2) as i:
                for n in range(2):
                    k = 3 * n
                    s = (k + 1) % 2
                    m = i * 2 + n
                    act.wait_ge(convolved, m + 1)
                    act.wait_ge(full[s], i * 3 + (FULL["sc_in"][s] + k // 2 + 1))
                    act_op(c_gate[n][:, :].rearrange("p (a b) -> p a b", a=TJ), result(s)).then_inc(taken[s], 1)
                    s = (k + 2) % 2
                    act.wait_ge(taken[s], i * 3 + (FREE["sc_in"][s] + (k + 1) // 2 + 2))
                    samples(m, n, st_sc[:, ds(m, 1), :, :].rearrange("p o b t -> p (o b) t"),
                            new_sc[:, ds(m, 1), :].rearrange("p o t -> p (o t)"))
            act.wait_ge(smp_full, 4 * KC)
            act.dma_start(conv_out, new_sc[:, :, :]).then_inc(stored, 16)
            act.wait_ge(full[0], FULL["sc_out"][0])
            act.wait_ge(taken[1], FREE["sc_out"][1] + 1)
            split_mixed(lambda: act.wait_ge(taken[0], FREE["sc_out"][0] + 1))
            norm(1, "sc_out", 0, False)
            act.preload_act_table(ACT.Silu)
            ffn(0)
            norm(2, "ffn0", FFN_OUT - KC, False)

            act.wait_ge(negated, 2)
            act.wait_ge(stored, 32)
            act.preload_act_table(ACT.Sigmoid)
            with act.Fori(0, KC) as c:
                def new_tokens(dst, src):
                    act_op(dst[:, ds(c, 1), :].rearrange("p o t -> p (o t)"), src[:, SEQ:T]).then_inc(new_copied, 1)

                def sigmoids(j):
                    i, h = STEPS[j]
                    width = P * (i + 1)
                    act.wait_ge(scored, c * N_STEPS + (j + 1))
                    if j >= 2:
                        act.wait_ge(turn_done, c * N_UNITS + turned_by(j - 2))
                    act_op(beta[j % 2][:, 0:width], score[j % 2][:, 0:width], ACT.Sigmoid,
                           bias=bias_pair[:, 0, h:h + 1]).then_inc(beta_done, 1)
                    act.wait_ge(scanned, c * N_STEPS + (j + 1))
                    act_op(keep[j % 2][:, 0:width], score[j % 2][:, 0:width], ACT.Sigmoid, scale=-1.0,
                           bias=bias_pair[:, 1, h:h + 1]).then_inc(keep_done, 1)

                def copy_turned(u):
                    act.wait_ge(turn_done, c * N_UNITS + (u + 1))
                    if u >= W_T:
                        act.wait_ge(pv_done, c * N_UNITS + (u - W_T + 1))
                    n = UNITS[u][2]
                    act_op(w_t[u % W_T][:, 0:n, :].rearrange("p a b -> p (a b)"),
                           turned[u % 2][:, 0:n * P]).then_inc(w_t_by_act, 1)

                act.wait_ge(taken[0], c * 3 + (FREE["qkv"][0] + 2))
                act_op(bias_pair[:, :, :], bias_h[:, :, ds(c * 2, 2)]).then_inc(pair_bias_set, 1)
                new_tokens(q_s, q_t)
                act.wait_ge(taken[1], c * 2 + (FREE["qkv"][1] + 2))
                act.dma_start(k_out[ds(c, 1), :, :].rearrange("o p t -> p (o t)"), k_t[:, :]).then_inc(kv_stored, 16)
                new_tokens(k_s, k_t)
                act.wait_ge(new_copied, c * 3 + 2)
                act.wait_ge(pair_bias_set, c + 1)
                sigmoids(0)
                sigmoids(1)
                act.wait_ge(taken[0], c * 3 + (FREE["qkv"][0] + 3))
                act.dma_start(v_out[ds(c, 1), :, :].rearrange("o p t -> p (o t)"), v_t[:, :]).then_inc(kv_stored, 16)
                new_tokens(v_s, v_t)
                act.wait_ge(v_turned, c + 1)
                act_op(v_rows[:, :, :].rearrange("p a b -> p (a b)"), attended).then_inc(v_ready, 1)
                for j in range(N_STEPS):
                    if BY_ACT[first_unit(j)]:
                        copy_turned(first_unit(j))
                    if j + 2 < N_STEPS:
                        sigmoids(j + 2)
                act.wait_ge(pv_done, c * N_UNITS + N_UNITS)
                act_op(mixed[:, ds(c, 1), SEQ // 2:SEQ].rearrange("p o t -> p (o t)"),
                       attended[:, SEQ // 2:SEQ]).then_inc(taken[1], 1)
                act.wait_ge(kv_stored, c * 32 + 32)
                act.wait_ge(new_copied, c * 3 + 3)
                act.sem_inc(kv_free, 1)
            def sample_sigmoids(bp):
                act.wait_ge(s_scored, bp + 3)
                z = out[1][:, bp % 2, 0:PAST + NS]
                act_op(beta_s[bp % 2][:, :], z, ACT.Sigmoid, bias=bias_r[:, 0:1]).then_inc(s_beta, 1)
                act_op(keep_s[bp % 2][:, :], z, ACT.Sigmoid, scale=-1.0, bias=bias_r[:, 1:2]).then_inc(s_keep, 1)

            def sample_rows(bp):
                act.wait_ge(s_full, bp + 3)
                act_op(o_rows[:, :], attended).then_inc(s_o_rows, 1)

            sample_sigmoids(0)
            for bp in range(NB // 2):
                if bp + 1 < NB // 2:
                    sample_sigmoids(bp + 1)
                sample_rows(bp)
            act.wait_ge(s_out, NB // 2 + 1)
            split_mixed()
            norm(3, "wo", 0, False)
            act.preload_act_table(ACT.Silu)
            ffn(1)
            norm(4, "ffn1", FFN_OUT - KC, False)
            for j in range(TJ):
                act.wait_ge(y_made, Y_BY_DVE * (j + 1))
                act.wait_ge(y_by_pool, (KC - Y_BY_DVE) * (j + 1))
                act.dma_start(y_out[:, :, j * TW:(j + 1) * TW].rearrange("f p t -> p f t"),
                              y_rows[:, :, j * TW:(j + 1) * TW]).then_inc(stored, 16)
            act.wait_ge(stored, 16 * (3 + TJ))
            act.wait_ge(kv_stored, 32 * KC)

        @block.vector
        def _(dve):
            V = nc.vector

            for s in range(2):
                dve.sem_inc(taken[s], 1)
            dve.sem_inc(scanned, 2)
            dve.sem_inc(keep_done, 2)
            dve.sem_inc(kv_free, 1)
            dve.sem_inc(s_out, 1)
            dve.sem_inc(a_ready, 2)
            dve.sem_inc(weighed, 1)
            V.memset(mean[:, :], 1.0 / D).then_inc(made, 1)
            V.memset(eps[:, :], EPS).then_inc(made, 1)
            for n in range(2):
                V.memset(ext[n][:, 0:CW - 1], 0.0).then_inc(made, 1)

            def wide(t):
                return t.rearrange("p (a b) -> p a b", a=TJ)

            def norm(nth, add, h_first):
                def low(f):
                    dve.wait_ge(h_high, H_BASE[nth] + f + 1)
                    V.scalar_tensor_tensor(h_lo[:, f, :], x[:, f, :], gain[:, nth, f:f + 1],
                                           h_hi[:, f, :].bitcast(f32), ALU.mult, ALU.subtract).then_inc(h_ready, 1)

                def sum_up(f):
                    n = KC * nth + f
                    dve.wait_ge(squared, n + 1)
                    if f == 0:
                        V.tensor_copy(total[:, :], square[0][:, :]).then_inc(summed, 1)
                    else:
                        dve.wait_ge(summed, n)
                        V.tensor_tensor(total[:, :], total[:, :], square[f % 2][:, :], ALU.add).then_inc(summed, 1)

                for f in range(KC):
                    add(f)
                    if h_first and f:
                        low(f - 1)
                    elif nth in (2, 4) and f:
                        sum_up(f - 1)
                    elif nth in (1, 3) and f < KC - 1:
                        sum_up(f)
                if h_first:
                    low(KC - 1)
                    for f in range(KC):
                        sum_up(f)
                elif nth == 2:
                    sum_up(KC - 1)
                    for f in range(KC):
                        low(f)
                else:
                    if nth < 4:
                        for f in range(KC):
                            low(f)
                    sum_up(KC - 1)
                if nth == 4:
                    return
                dve.wait_ge(taken[0], FREE[f"norm{nth}"][0] + 2)
                V.reciprocal(rstd[:, :], total[:, :]).then_inc(rstd_made, 1)
                dve.wait_ge(rstd_made, nth + 1)

            H_BASE = {0: H_SC_IN, 1: H_FFN0, 2: H_QKV, 3: H_FFN1}

            def split_mixed(h_base):
                for f in range(KC):
                    dve.wait_ge(h_high, h_base + f + 1)
                    V.tensor_tensor(h_lo[:, f, :], mixed[:, f, :], h_hi[:, f, :].bitcast(f32),
                                    ALU.subtract).then_inc(h_ready, 1)

            def conv(m, par, tap):
                e, o = ext[par], y[par]
                V.tensor_scalar(o[:, 0:SEQ], e[:, 0:SEQ], tap(0), None, ALU.mult).then_inc(tapped, 1)
                dve.wait_ge(smp_full, m * 4 + 2)
                q, r = smp[par], y[par][:, SEQ:T].rearrange("p (b t) -> p b t", t=NT)
                V.tensor_scalar(r, q[:, :, 0:NT], tap(0), None, ALU.mult).then_inc(tapped, 1)
                for n in range(1, CW):
                    dve.wait_ge(tapped, m * 4 + (2 * n - 1))
                    main = V.scalar_tensor_tensor(o[:, 0:SEQ], e[:, n:n + SEQ], tap(n), o[:, 0:SEQ], ALU.mult, ALU.add)
                    if n < CW - 1:
                        main.then_inc(tapped, 1)
                    dve.wait_ge(tapped, m * 4 + 2 * n)
                    if n == CW - 1:
                        dve.wait_ge(smp_full, m * 4 + 4)
                    last = V.scalar_tensor_tensor(r, q[:, :, n:n + NT], tap(n), r, ALU.mult, ALU.add)
                    if n < CW - 1:
                        last.then_inc(tapped, 1)
                last.then_inc(convolved, 1)

            def ffn_chunk(m, par, chunk, layer, k, trip, slot):
                name = f"ffn{layer}"
                s = (k + 1) % 2
                dve.wait_ge(convolved, m + 1)
                dve.wait_ge(full[s], trip * TRIP_FILLS + (FULL[name][s] + k // 2 + 1))
                V.tensor_tensor(wide(ext[par][:, CW - 1:]), result(s), wide(rstd[:, :]), ALU.mult).then_inc(taken[s], 1)
                dve.wait_ge(taken[s], trip * TRIP_FILLS + (FREE[name][s] + k // 2 + 2))
                dve.wait_ge(a_ready, m - (KC - 1))
                conv(m, par, lambda t: tap_ffn[:, ds(chunk + layer * FC, 1), t:t + 1].rearrange("p o t -> p (o t)"))
                s = (k + 2) % 2
                dve.wait_ge(silued, m - (KC - 1))
                V.tensor_tensor(y[par][:, :], y[par][:, :], rstd[:, :], ALU.mult).then_inc(y_scaled, 1)
                dve.wait_ge(y_scaled, m + 1)
                dve.wait_ge(full[s], trip * TRIP_FILLS + (FULL[name][s] + (k + 1) // 2 + 1))
                yy = wide(y[par][:, :])
                V.tensor_tensor(yy, yy, result(s), ALU.mult).then_inc(taken[s], 1)
                dve.wait_ge(a_high, m - (KC - 1))
                V.tensor_tensor(a_lo[:, slot, par, :], y[par][:, :], a_hi[:, slot, par, :].bitcast(f32),
                                ALU.subtract).then_inc(a_ready, 1)

            def add_x(f, name, k, trip):
                s = (k + 1) % 2
                dve.wait_ge(full[s], trip * TRIP_FILLS + (FULL[name][s] + k // 2 + 1))
                xx = x[:, f, :].rearrange("p (a b) -> p a b", a=TJ)
                V.tensor_tensor(xx, xx, result(s), ALU.add).then_inc(taken[s], 1)

            def ffn(layer):
                name = f"ffn{layer}"
                m0 = M_FFN[layer]

                def up(m, chunk, k0, trip, slot):
                    for p in range(2):
                        ffn_chunk(m + p, p, chunk + p, layer, k0 + 2 * p, trip, slot)

                def down(k0, trip):
                    for f in range(KC):
                        add_x(f, name, k0 + f, trip)

                up(m0, 0, 0, 0, 0)
                with dve.Fori(0, FFN_TRIPS) as i:
                    for n in range(2):
                        k0 = (4 + KC) * n + 4
                        up(i * 4 + (m0 + 2 + 2 * n), i * 4 + (2 + 2 * n), k0, i, (n + 1) % 2)
                        down(k0 + 4, i)
                return lambda f: add_x(f, name, FFN_OUT - KC + f, 0)

            dve.wait_ge(gain_loaded, 16)
            norm(0, lambda f: dve.wait_ge(x_loaded[f], 16), True)
            dve.wait_ge(consts, 16 * 8)
            dve.wait_ge(made, 4)
            V.tensor_tensor(rstd2[:, :], rstd[:, :], rstd[:, :], ALU.mult).then_inc(squared_rstd, 1)
            dve.wait_ge(squared_rstd, 1)
            with dve.Fori(0, KC // 2) as i:
                for n in range(2):
                    m = i * 2 + n
                    k = 3 * n + 1
                    s = (k + 1) % 2
                    dve.wait_ge(convolved, m + 1)
                    gate = (k + 2) % 2
                    dve.wait_ge(taken[gate], i * 3 + (FREE["sc_in"][gate] + (k - 1) // 2 + 2))
                    V.tensor_tensor(c_gate[n][:, :], c_gate[n][:, :], rstd2[:, :], ALU.mult).then_inc(c_scaled, 1)
                    dve.wait_ge(c_scaled, m + 1)
                    dve.wait_ge(full[s], i * 3 + (FULL["sc_in"][s] + k // 2 + 1))
                    V.tensor_tensor(ext[n][:, CW - 1:].rearrange("p (a b) -> p a b", a=TJ),
                                    c_gate[n][:, :].rearrange("p (a b) -> p a b", a=TJ), result(s),
                                    ALU.mult).then_inc(taken[s], 1)
                    dve.wait_ge(taken[s], i * 3 + (FREE["sc_in"][s] + k // 2 + 2))
                    conv(m, n, lambda t: tap_sc[:, ds(m, 1), t:t + 1].rearrange("p o t -> p (o t)"))
                    k = 3 * n + 2
                    s = (k + 1) % 2
                    dve.wait_ge(convolved, m + 3)
                    V.tensor_tensor(y[n][:, :], y[n][:, :], rstd[:, :], ALU.mult).then_inc(y_scaled, 1)
                    dve.wait_ge(y_scaled, m + 1)
                    dve.wait_ge(full[s], i * 3 + (FULL["sc_in"][s] + k // 2 + 1))
                    V.tensor_tensor(mixed[:, ds(m, 1), :].rearrange("p o (a b) -> p (o a) b", a=TJ),
                                    y[n][:, :].rearrange("p (a b) -> p a b", a=TJ), result(s),
                                    ALU.mult).then_inc(taken[s], 1)
            split_mixed(H_SC_OUT)
            norm(1, lambda f: add_x(f, "sc_out", f, 0), False)
            last_add = ffn(0)
            norm(2, last_add, False)

            with dve.Fori(0, KC) as c:
                def take(dst, s, full_nth, scale=None):
                    dve.wait_ge(full[s], full_nth + 1)
                    if scale is None:
                        V.tensor_tensor(wide(dst[:, :]), result(s), wide(rstd[:, :]), ALU.mult).then_inc(taken[s], 1)
                    else:
                        V.scalar_tensor_tensor(wide(dst[:, :]), result(s), scale, wide(rstd[:, :]),
                                               ALU.mult, ALU.mult).then_inc(taken[s], 1)

                def copy_turned(u):
                    dve.wait_ge(turn_done, c * N_UNITS + (u + 1))
                    if u >= W_T:
                        dve.wait_ge(pv_done, c * N_UNITS + (u - W_T + 1))
                    n = UNITS[u][2]
                    V.tensor_copy(w_t[u % W_T][:, 0:n, :].rearrange("p a b -> p (a b)"),
                                  turned[u % 2][:, 0:n * P]).then_inc(w_t_by_dve, 1)

                def weigh(j):
                    i = STEPS[j][0]
                    width = P * (i + 1)
                    dve.wait_ge(beta_done, c * N_STEPS + (j + 1))
                    dve.wait_ge(keep_done, c * N_STEPS + (j + 3))
                    dve.wait_ge(weighed, c * N_STEPS + (j + 1))
                    back = keep[j % 2][:, width - 1:0:-1]
                    V.tensor_tensor_scan(prod[:, width - 1:0:-1], back, back, 1.0,
                                         ALU.mult, ALU.bypass).then_inc(scanned, 1)
                    dve.wait_ge(scanned, c * N_STEPS + (j + 3))
                    V.tensor_tensor(beta[j % 2][:, 0:width - 1], beta[j % 2][:, 0:width - 1], prod[:, 1:width],
                                    ALU.mult).then_inc(weighed, 1)

                dve.wait_ge(kv_free, c + 1)
                take(q_t, 0, c * 2 + FULL["qkv"][0], DH ** -0.5)
                take(k_t, 1, c + FULL["qkv"][1])
                weigh(0)
                weigh(1)
                take(v_t, 0, c * 2 + (FULL["qkv"][0] + 1))
                for u in range(N_UNITS):
                    if not BY_ACT[u]:
                        copy_turned(u)
                    j, first, _ = UNITS[u]
                    if u + 1 < N_UNITS and UNITS[u + 1][0] == j + 1 and j + 2 < N_STEPS:
                        weigh(j + 2)
                dve.wait_ge(pv_done, c * N_UNITS + N_UNITS)
                V.tensor_copy(mixed[:, ds(c, 1), 0:SEQ // 2].rearrange("p o t -> p (o t)"),
                              attended[:, 0:SEQ // 2]).then_inc(taken[0], 1)

            dve.wait_ge(kv_free, KC + 1)
            for n in range(2):
                V.memset(q_rows[n][:, :], 0.0).then_inc(made, 1)
            dve.wait_ge(made, 6)

            def sample_q(bp):
                if bp >= 2:
                    dve.wait_ge(s_scored, bp + 1)
                for h in range(2):
                    rows = slice(DH * h, DH * h + DH)
                    o = q_rows[bp % 2][rows, :].rearrange("p (c r) -> p c r", c=KC)[:, :, 0:P]
                    o = o.rearrange("p c (b r) -> p c b r", b=2)[:, :, :, h * NT:(h + 1) * NT]
                    q = q_s[rows, :, bp * 2 * NT:(bp + 1) * 2 * NT].rearrange("p c (b t) -> p c b t", b=2)
                    last = V.tensor_copy(o, q)
                last.then_inc(s_set, 1)

            def sample_weigh(bp):
                dve.wait_ge(s_beta, bp + 1)
                dve.wait_ge(s_keep, bp + 1)
                if bp:
                    dve.wait_ge(s_weighed, bp)
                n, w, back = PAST + NS, beta_s[bp % 2], keep_s[bp % 2][:, PAST + NS - 1:0:-1]
                V.tensor_tensor_scan(prod_s[:, n - 1:0:-1], back, back, 1.0, ALU.mult, ALU.bypass).then_inc(s_scan, 1)
                dve.wait_ge(s_scan, bp + 1)
                V.tensor_tensor(w[:, 0:n - 1], w[:, 0:n - 1], prod_s[:, 1:n], ALU.mult).then_inc(s_weighed, 1)

            def sample_copy(bp):
                dve.wait_ge(s_turned, bp + 1)
                V.tensor_copy(w_ts[:, 0:PAGES, :].rearrange("p a b -> p (a b)"), out[1][:, 2, 0:PAST])
                V.tensor_copy(w_ts[0:NS, PAGES, :], out[1][0:NS, 2, PAST:PAST + P]).then_inc(s_wt, 1)

            def sample_take(bp):
                dve.wait_ge(s_o_turned, bp + 1)
                for h in range(2):
                    rows = slice(DH * h, DH * h + DH)
                    o = mixed[rows, :, SEQ + bp * 2 * NT:SEQ + (bp + 1) * 2 * NT].rearrange("p c (b t) -> p c b t", b=2)
                    r = score[1][rows, :].rearrange("p (c b r) -> p c b r", c=KC, b=2)
                    for c in range(KC):
                        last = V.tensor_copy(o[:, c, :, :], r[:, c, :, 8 * c + 4 * h:8 * c + 4 * h + NT])
                last.then_inc(s_out, 1)

            sample_q(0)
            dve.wait_ge(s_vturned, 1)
            V.tensor_copy(v_new[:, :], score[1][0:NS, :]).then_inc(s_vnew, 1)
            sample_q(1)
            sample_weigh(0)
            for bp in range(NB // 2):
                sample_copy(bp)
                if bp + 2 < NB // 2:
                    sample_q(bp + 2)
                if bp + 1 < NB // 2:
                    sample_weigh(bp + 1)
                if bp:
                    sample_take(bp - 1)
            sample_take(NB // 2 - 1)
            for n in range(2):
                V.memset(ext[n][:, 0:CW - 1], 0.0).then_inc(made, 1)
            dve.wait_ge(made, 8)
            split_mixed(H_WO)
            norm(3, lambda f: add_x(f, "wo", f, 0), False)
            last_add = ffn(1)
            norm(4, last_add, False)
            for j in range(TJ):
                block = slice(j * TW, (j + 1) * TW)
                dve.wait_ge(root_made, j + 1)
                V.reciprocal(rstd[:, block], total[:, block]).then_inc(rstd_made, 1)
                dve.wait_ge(rstd_made, 4 + j + 1)
                for f in range(Y_BY_DVE):
                    if j == 0:
                        dve.wait_ge(y_gained, f + 1)
                    V.tensor_tensor(y_rows[:, f, block], y_rows[:, f, block], rstd[:, block], ALU.mult).then_inc(y_made, 1)


def kernel(**inputs):
    import numpy as np
    import ml_dtypes
    import concourse.bacc as bacc
    from concourse.bass_utils import run_bass_kernel_spmd

    a = {k: np.asarray(v) for k, v in inputs.items()}

    def by_features(v):
        v = v.reshape(v.shape[:-1] + (v.shape[-1] // P, P))
        return np.moveaxis(np.moveaxis(v, -1, 0), -1, 1)

    def tiles(w, order):
        k, n = w.shape
        t = w.reshape(k // P, P, n // P, P).transpose(2, 1, 0, 3).reshape(n // P, P, k)
        return t[order]

    tokens = np.concatenate([a["x_prompt"].reshape(SEQ, D), a["x_sample"].reshape(NS, D)])
    chunks = np.arange(KC)
    sc_in = tiles(a["w_sc_in"][0], np.stack([KC + chunks, 2 * KC + chunks, chunks], 1).ravel())
    qkv = tiles(a["w_qkv"][0], np.stack([chunks, KC + chunks, 2 * KC + chunks], 1).ravel())

    def ffn(layer):
        hidden = np.arange(FC)
        up = tiles(a["w_ffn_up"][layer], np.stack([hidden, FC + hidden], 1).ravel())
        down = a["w_ffn_down"][layer].reshape(FC, P, D)
        rows = [up[0:4]]
        for g in range(1, PAIRS):
            rows += [up[4 * g:4 * g + 4], down[2 * g - 2:2 * g]]
        return rows + [down[FC - 2:]]

    weights = np.concatenate([sc_in, tiles(a["w_sc_out"][0], chunks), *ffn(0), qkv,
                              tiles(a["w_o"][0], chunks), *ffn(1)])
    gains = np.concatenate([np.stack([a["norm_mix"][0], a["norm_ffn"][0], a["norm_mix"][1], a["norm_ffn"][1],
                                      a["norm_final"]])])
    taps_sc = np.concatenate([a["w_sc_dw"][0], np.zeros((1, D), np.float32)])
    taps_ffn = np.concatenate([a["w_ffn_dw"], a["b_ffn_dw"][:, None, :]], 1)
    bf16 = ml_dtypes.bfloat16
    key, query = np.arange(P)[None, :], np.arange(P)[:, None]
    mask_diag = np.where(key < query, 0.0, MASKED).astype(bf16)
    row, new = np.arange(P)[:, None, None], np.arange(NS)[None, None, :]
    sample = 2 * np.arange(NB // 2)[None, :, None] + row // (P // 2)
    mask_new = np.where((new // NT == sample) & (new % NT < row % NT), 0.0, MASKED).astype(bf16)
    pool = a["cache_k"].shape[1]
    arrays = {
        "x_in": tokens.T.reshape(KC, P, T),
        "weights": weights,
        "taps_sc": by_features(taps_sc),
        "taps_ffn": by_features(taps_ffn).transpose(0, 2, 1, 3).reshape(P, 2 * FC, CW + 1),
        "state_sc": by_features(a["state_conv"][0]),
        "state_ffn": by_features(a["state_ffn"]).transpose(0, 2, 1, 3, 4).reshape(P, 2 * FC, NB, CW - 1),
        "gains": by_features(gains).transpose(0, 2, 1),
        "bias_heads": np.repeat(a["sb_bias"].reshape(1, H), P, 0),
        "bias_rows": np.tile(np.repeat(a["sb_bias"].reshape(H), NT), 2).reshape(P, 1),
        "cache_k": a["cache_k"][0].reshape(pool, PG, KC, P).transpose(0, 3, 2, 1),
        "cache_v": a["cache_v"][0].reshape(pool, PG, D),
        "pages": a["page_table"].reshape(1, NB * PAGES),
        "mask_diag": mask_diag,
        "mask_new": mask_new,
        "ident_in": np.eye(P, dtype=np.float32),
        "ident_b_in": np.eye(P, dtype=bf16),
    }
    arrays = {k: np.ascontiguousarray(v) for k, v in arrays.items()}
    outs = {"y_out": (KC, P, T), "k_out": (KC, P, T), "v_out": (KC, P, T),
            "conv_out": (P, KC, (1 + NB) * (CW - 1)), "ffn_out": (2, P, FC, (1 + NB) * (CW - 1))}
    nc = bacc.Bacc("TRN2", target_bir_lowering=False, num_devices=1, dynamic_dma_scratch_size=1024)
    args = {k: nc.dram_tensor(k, v.shape, mybir.dt.from_np(v.dtype), kind="ExternalInput").ap()
            for k, v in arrays.items()}
    args |= {k: nc.dram_tensor(k, shape, mybir.dt.float32, kind="ExternalOutput").ap() for k, shape in outs.items()}
    build(nc, **args)
    got = run_bass_kernel_spmd(nc, [arrays], core_ids=[0]).results[0]

    def by_tokens(v):
        v = v.reshape(D, T).T
        return v[:SEQ], v[SEQ:]

    y_p, y_s = by_tokens(got["y_out"])
    k_p, k_s = by_tokens(got["k_out"])
    v_p, v_s = by_tokens(got["v_out"])

    def states(v):
        v = v.transpose(2, 1, 0).reshape((1 + NB) * (CW - 1), -1)
        return v[:CW - 1], v[CW - 1:].reshape(NB, CW - 1, -1)

    conv_p, conv_s = states(got["conv_out"])
    ffn_p, ffn_s = zip(*(states(v) for v in got["ffn_out"]), strict=True)
    return (y_p.reshape(1, SEQ, D), y_s.reshape(NB, NT, D),
            k_p.reshape(1, 1, SEQ, H, DH), v_p.reshape(1, 1, SEQ, H, DH),
            conv_p[None, None], np.stack(ffn_p)[:, None],
            k_s.reshape(1, NB, NT, H, DH), v_s.reshape(1, NB, NT, H, DH),
            conv_s[None], np.stack(ffn_s))
```
